# Optimizing a Trainium2 kernel written in Bass

```python
import jax, jax.numpy as jnp
from jax import lax
import numpy as np

D_MODEL = 2048
BATCH = 1
SEQ = 256
DEPTH = 2

EPS = 1e-6
LRU_HEADS = 12
LRU_HEAD_DIM = 128
LRU_WIDTH = LRU_HEADS * LRU_HEAD_DIM
CONV_WIDTH = 4
LRU_C = 8.0
DIL_PATTERNS = ((128, 1), (512, 4), (2048, 16))
N_DIL = 3
ATT_HEADS_PER_GROUP = 4
ATT_HEAD_DIM = 128
ATT_HEADS = N_DIL * ATT_HEADS_PER_GROUP
ATT_WIDTH = ATT_HEADS * ATT_HEAD_DIM
ATT_OUT = ATT_HEADS_PER_GROUP * ATT_HEAD_DIM
EVEN_SIZES = (LRU_WIDTH, LRU_WIDTH, ATT_WIDTH, ATT_WIDTH, ATT_WIDTH, ATT_OUT)
EVEN_IN = 2 * LRU_WIDTH + 3 * ATT_WIDTH + ATT_OUT
EVEN_OUT = LRU_WIDTH + ATT_OUT
GLA_HEADS = 4
GLA_DK = 128
GLA_DV = 256
GLA_KW = GLA_HEADS * GLA_DK
GLA_VW = GLA_HEADS * GLA_DV
GLA_RANK = 16
GLA_TAU = 16.0
GLA_CHUNK = 64
SG_GROUPS = 4
SG_GROUP_DIM = 256
SG_WIDTH = SG_GROUPS * SG_GROUP_DIM
SG_CHUNK = 128
ODD_SIZES = (GLA_KW, GLA_KW, GLA_VW, GLA_RANK, GLA_VW, SG_WIDTH, SG_WIDTH, SG_WIDTH)
ODD_IN = 2 * GLA_KW + 2 * GLA_VW + GLA_RANK + 3 * SG_WIDTH
ODD_OUT = GLA_VW + SG_WIDTH


F32 = jnp.float32

def split_points(sizes):
    pts, acc = [], 0
    for s in sizes[:-1]:
        acc += s
        pts.append(acc)
    return pts

def rms_norm(x, g):
    xf = x.astype(F32)
    y = xf * lax.rsqrt(jnp.mean(xf * xf, axis=-1, keepdims=True) + EPS)
    return (y * g.astype(F32)).astype(x.dtype)

def causal_conv(x, w, b):
    k_w = w.shape[0]
    seq = x.shape[1]
    xp = jnp.pad(x, ((0, 0), (k_w - 1, 0), (0, 0)))
    return sum(xp[:, j:j + seq] * w[j] for j in range(k_w)) + b

def _lru_combine(left, right):
    a_l, h_l = left
    a_r, h_r = right
    return a_l * a_r, a_r * h_l + h_r

def rg_lru(x, w_a, b_a, w_i, b_i, lam):
    bsz, seq, width = x.shape
    xf = x.astype(F32)
    xh = xf.reshape(bsz, seq, LRU_HEADS, LRU_HEAD_DIM)
    r = jax.nn.sigmoid(jnp.einsum('bshi,hij->bshj', xh, w_a.astype(F32)) + b_a.astype(F32))
    i = jax.nn.sigmoid(jnp.einsum('bshi,hij->bshj', xh, w_i.astype(F32)) + b_i.astype(F32))
    r = r.reshape(bsz, seq, width)
    i = i.reshape(bsz, seq, width)
    log_a = -LRU_C * r * jax.nn.softplus(-lam.astype(F32))
    a = jnp.exp(log_a)
    u = jnp.sqrt(-jnp.expm1(2.0 * log_a)) * (i * xf)
    _, hs = lax.associative_scan(_lru_combine, (a, u), axis=1)
    return hs.astype(x.dtype)

def alibi_slopes():
    g = np.arange(N_DIL)[:, None]
    j = np.arange(ATT_HEADS_PER_GROUP)[None, :]
    return jnp.asarray(2.0 ** (-8.0 * (g + N_DIL * j + 1) / ATT_HEADS), F32)

def dilated_group(q, k, v, dil, sub_w, slopes):
    bsz, seq, nh, dh = q.shape
    L = seq // dil
    nb = -(-L // sub_w)
    Lp = nb * sub_w

    def strided(t):
        t = t.reshape(bsz, L, dil, nh, dh).transpose(0, 2, 3, 1, 4)
        return jnp.pad(t, ((0, 0), (0, 0), (0, 0), (0, Lp - L), (0, 0)))

    def banded(t):
        t = jnp.pad(t, ((0, 0), (0, 0), (0, 0), (sub_w, 0), (0, 0)))
        t = t.reshape(bsz, dil, nh, nb + 1, sub_w, dh)
        return jnp.concatenate([t[:, :, :, :-1], t[:, :, :, 1:]], axis=-2)

    qb = strided(q).reshape(bsz, dil, nh, nb, sub_w, dh)
    kb = banded(strided(k))
    vb = banded(strided(v))
    s = jnp.einsum('brhnqe,brhnke->brhnqk', qb, kb) * (dh ** -0.5)
    qi = jnp.arange(sub_w)[:, None]
    ki = jnp.arange(2 * sub_w)[None, :]
    delta = sub_w + qi - ki
    blk = jnp.arange(nb)[:, None, None]
    valid = (delta >= 0) & (delta <= sub_w) & (blk * sub_w - sub_w + ki >= 0)
    dist = (delta * dil).astype(F32)
    s = s - slopes[None, None, :, None, None, None] * dist
    s = jnp.where(valid, s, -jnp.inf)
    m = jnp.max(s, axis=-1, keepdims=True)
    p = jnp.exp(s - m)
    den = jnp.sum(p, axis=-1, keepdims=True)
    o = jnp.einsum('brhnqk,brhnke->brhnqe', p, vb) / den
    lse = (m + jnp.log(den))[..., 0]

    def unstrided(t):
        t = t.reshape(bsz, dil, nh, Lp, *t.shape[5:])[:, :, :, :L]
        t = jnp.moveaxis(t, 3, 1)
        return t.reshape(bsz, seq, nh, *t.shape[4:])

    return unstrided(o), unstrided(lse)

def dilated_attention(q, k, v):
    bsz, seq, _ = q.shape
    shape = (bsz, seq, N_DIL, ATT_HEADS_PER_GROUP, ATT_HEAD_DIM)
    qh, kh, vh = (t.astype(F32).reshape(shape) for t in (q, k, v))
    slopes = alibi_slopes()
    outs, lses = [], []
    for g, (win, dil) in enumerate(DIL_PATTERNS):
        o, l = dilated_group(qh[:, :, g], kh[:, :, g], vh[:, :, g], dil, win // dil, slopes[g])
        outs.append(o)
        lses.append(l)
    wts = jax.nn.softmax(jnp.stack(lses, axis=0), axis=0)
    y = jnp.einsum('gbsh,gbshe->bshe', wts, jnp.stack(outs, axis=0))
    return y.reshape(bsz, seq, ATT_OUT).astype(q.dtype)

def gla_chunked(q, k, v, log_a):
    bsz, seq, nh, dk = q.shape
    dv = v.shape[-1]
    nc = seq // GLA_CHUNK

    def chunks(t):
        return t.astype(F32).reshape(bsz, nc, GLA_CHUNK, nh, t.shape[-1]).transpose(0, 3, 1, 2, 4)

    q, k, v, log_a = chunks(q), chunks(k), chunks(v), chunks(log_a)
    q = q * (dk ** -0.5)
    b = jnp.cumsum(log_a, axis=3)
    b_last = b[:, :, :, -1:, :]
    qt = q * jnp.exp(b)
    kt = k * jnp.exp(-b)
    causal = jnp.tril(jnp.ones((GLA_CHUNK, GLA_CHUNK), bool))
    att = jnp.where(causal, jnp.einsum('bhnie,bhnje->bhnij', qt, kt), 0.0)
    o_intra = jnp.einsum('bhnij,bhnjv->bhniv', att, v)
    upd = jnp.einsum('bhnje,bhnjv->bhnev', k * jnp.exp(b_last - b), v)
    decay = jnp.exp(b_last[:, :, :, 0, :])

    def step(state, inp):
        dec, u = inp
        return dec[..., None] * state + u, state

    init = jnp.zeros((bsz, nh, dk, dv), F32)
    _, s_prev = lax.scan(step, init, (jnp.moveaxis(decay, 2, 0), jnp.moveaxis(upd, 2, 0)))
    o_inter = jnp.einsum('bhnie,nbhev->bhniv', qt, s_prev)
    o = o_intra + o_inter
    return o.transpose(0, 2, 3, 1, 4).reshape(bsz, seq, nh, dv)

def spatial_gating(u, v, w_s, b_s, v_norm):
    bsz, seq, _ = u.shape
    nc = seq // SG_CHUNK
    vf = v.astype(F32).reshape(bsz, nc, SG_CHUNK, SG_GROUPS, SG_GROUP_DIM)
    mu = jnp.mean(vf, axis=-1, keepdims=True)
    var = jnp.mean(jnp.square(vf - mu), axis=-1, keepdims=True)
    vf = (vf - mu) * lax.rsqrt(var + EPS) * v_norm.astype(F32)
    mask = jnp.tril(jnp.ones((SG_CHUNK, SG_CHUNK), bool))
    w = jnp.where(mask, w_s.astype(F32), 0.0)
    s = jnp.einsum('gts,bcsge->bctge', w, vf) + b_s.astype(F32).T[:, :, None]
    return (u.astype(F32) * s.reshape(bsz, seq, SG_WIDTH)).astype(u.dtype)

def even_layer(x, norm, w_in, conv_w, conv_b, w_a, b_a, w_i, b_i, lam, w_out):
    h = rms_norm(x, norm)
    z = h @ w_in
    xa, ga, q, k, v, gb = jnp.split(z, split_points(EVEN_SIZES), axis=-1)
    ya = rg_lru(causal_conv(xa, conv_w, conv_b), w_a, b_a, w_i, b_i, lam) * jax.nn.silu(ga)
    yb = dilated_attention(q, k, v) * jax.nn.silu(gb)
    return jnp.concatenate([ya.astype(x.dtype), yb.astype(x.dtype)], axis=-1) @ w_out

def odd_layer(x, norm, w_in, w_alpha, b_alpha, head_norm, v_norm, w_s, b_s, w_out):
    bsz, seq, _ = x.shape
    h = rms_norm(x, norm)
    z = h @ w_in
    q, k, v, a_lr, gc, u, vd, gd = jnp.split(z, split_points(ODD_SIZES), axis=-1)
    log_a = jax.nn.log_sigmoid((a_lr @ w_alpha + b_alpha).astype(F32)) / GLA_TAU

    def heads(t, e):
        return t.reshape(bsz, seq, GLA_HEADS, e)

    o = gla_chunked(heads(q, GLA_DK), heads(k, GLA_DK), heads(v, GLA_DV), heads(log_a, GLA_DK))
    yc = rms_norm(o, head_norm).reshape(bsz, seq, GLA_VW).astype(x.dtype) * jax.nn.silu(gc)
    yd = spatial_gating(jax.nn.gelu(u), jax.nn.gelu(vd), w_s, b_s, v_norm) * jax.nn.silu(gd)
    return jnp.concatenate([yc.astype(x.dtype), yd.astype(x.dtype)], axis=-1) @ w_out

def first_inputs(seed: int = 0) -> dict:
    key = jax.random.key(seed)
    ks = jax.random.split(key, 21)
    ne, no = (DEPTH + 1) // 2, DEPTH // 2

    def nrm(k, shape, scale):
        return scale * jax.random.normal(k, shape, F32)

    def gain(k, shape):
        return 1.0 + 0.02 * jax.random.normal(k, shape, F32)

    s_lru = jax.random.uniform(ks[9], (ne, LRU_WIDTH), F32, minval=0.9, maxval=0.999) ** (1.0 / LRU_C)
    return {
        'x': nrm(ks[0], (BATCH, SEQ, D_MODEL), 1.0),
        'ev_norm': gain(ks[1], (ne, D_MODEL)),
        'ev_w_in': nrm(ks[2], (ne, D_MODEL, EVEN_IN), D_MODEL ** -0.5),
        'ev_conv_w': nrm(ks[3], (ne, CONV_WIDTH, LRU_WIDTH), CONV_WIDTH ** -0.5),
        'ev_conv_b': nrm(ks[4], (ne, LRU_WIDTH), 0.01),
        'ev_w_a': nrm(ks[5], (ne, LRU_HEADS, LRU_HEAD_DIM, LRU_HEAD_DIM), LRU_HEAD_DIM ** -0.5),
        'ev_b_a': nrm(ks[6], (ne, LRU_HEADS, LRU_HEAD_DIM), 0.01),
        'ev_w_i': nrm(ks[7], (ne, LRU_HEADS, LRU_HEAD_DIM, LRU_HEAD_DIM), LRU_HEAD_DIM ** -0.5),
        'ev_b_i': nrm(ks[8], (ne, LRU_HEADS, LRU_HEAD_DIM), 0.01),
        'ev_lam': jnp.log(s_lru) - jnp.log1p(-s_lru),
        'ev_w_out': nrm(ks[10], (ne, EVEN_OUT, D_MODEL), EVEN_OUT ** -0.5),
        'od_norm': gain(ks[11], (no, D_MODEL)),
        'od_w_in': nrm(ks[12], (no, D_MODEL, ODD_IN), D_MODEL ** -0.5),
        'od_w_alpha': nrm(ks[13], (no, GLA_RANK, GLA_KW), GLA_RANK ** -0.5),
        'od_b_alpha': nrm(ks[14], (no, GLA_KW), 0.01),
        'od_head_norm': gain(ks[15], (no, GLA_HEADS, GLA_DV)),
        'od_v_norm': gain(ks[16], (no, SG_GROUPS, SG_GROUP_DIM)),
        'od_w_s': nrm(ks[17], (no, SG_GROUPS, SG_CHUNK, SG_CHUNK), SG_CHUNK ** -0.5),
        'od_b_s': 1.0 + nrm(ks[18], (no, SG_GROUPS, SG_CHUNK), 0.01),
        'od_w_out': nrm(ks[19], (no, ODD_OUT, D_MODEL), ODD_OUT ** -0.5),
        'final_norm': gain(ks[20], (D_MODEL,)),
    }

def first_block(x, ev_norm, ev_w_in, ev_conv_w, ev_conv_b, ev_w_a, ev_b_a, ev_w_i, ev_b_i, ev_lam,
              ev_w_out, od_norm, od_w_in, od_w_alpha, od_b_alpha, od_head_norm, od_v_norm,
              od_w_s, od_b_s, od_w_out, final_norm):
    for layer in range(DEPTH):
        i = layer // 2
        if layer % 2 == 0:
            x = x + even_layer(x, ev_norm[i], ev_w_in[i], ev_conv_w[i], ev_conv_b[i], ev_w_a[i],
                               ev_b_a[i], ev_w_i[i], ev_b_i[i], ev_lam[i], ev_w_out[i])
        else:
            x = x + odd_layer(x, od_norm[i], od_w_in[i], od_w_alpha[i], od_b_alpha[i],
                              od_head_norm[i], od_v_norm[i], od_w_s[i], od_b_s[i], od_w_out[i])
    return rms_norm(x, final_norm)


_first_inputs = first_inputs


def first_inputs(seed=0):
    import zlib

    import numpy as np

    out = dict(_first_inputs(seed))
    spreads = {}
    factors = {'ev_norm': 5.221,
     'ev_b_a': 37.14,
     'ev_b_i': 31.885,
     'od_norm': 3.345,
     'od_b_alpha': 60.458,
     'od_head_norm': 63.592,
     'od_v_norm': 47.142,
     'od_b_s': 64.0,
     'final_norm': 8.303,
     'ev_conv_b': 4.928}
    for name, (base, spread) in spreads.items():
        noise = np.random.default_rng([zlib.crc32(name.encode()), seed]).standard_normal(out[name].shape)
        drawn = base * np.exp(spread * noise) if base else spread * noise
        out[name] = __import__('jax').numpy.asarray(drawn.astype(out[name].dtype))
    for name, factor in factors.items():
        out[name] = (out[name] * factor).astype(out[name].dtype)
    return out


_narrow_inputs = first_inputs


def first_inputs(seed=0):

    out = dict(_narrow_inputs(seed))
    wider = {'od_head_norm': 8.85, 'od_v_norm': 7.79, 'od_b_s': 8.84, 'final_norm': 3.24}
    for name, times in wider.items():
        mean = out[name].mean()
        out[name] = (mean + times * (out[name] - mean)).astype(out[name].dtype)
    return out


N_EVEN = (DEPTH + 1) // 2
N_ODD = DEPTH // 2

A_HEADS = 8
A_DK = 128
A_DV = 128
A_QK = A_HEADS * A_DK
A_WIDTH = A_HEADS * A_DV
B_HEADS = 8
B_DK = 128
B_DV = 128
B_QK = B_HEADS * B_DK
B_WIDTH = B_HEADS * B_DV
CONV_K = 4
CHUNK = 64
EVEN_IN_2 = 2 * A_QK + 2 * A_WIDTH + 2 * B_QK + 2 * B_WIDTH + 2 * B_HEADS
EVEN_OUT_2 = A_WIDTH + B_WIDTH

C_HEADS = 16
C_GROUPS = 4
C_HPG = C_HEADS // C_GROUPS
C_DK = 128
C_DV = 128
C_Q = C_HEADS * C_DK
C_KV = C_GROUPS * C_DK
CMP_LEN = 32
CMP_STRIDE = 16
SEL_BLOCK = 64
N_SEL = 8
WINDOW = 512
Q_BLOCK = 128
SEL_Q_BLOCK = 64
SEL_FORCE = 1e4
ODD_IN_2 = C_Q + 6 * C_KV + 3 * C_HEADS
ODD_OUT_2 = C_HEADS * C_DV

D_FF = -(-8 * D_MODEL // (3 * 256)) * 256
NORM_EPS = 1e-6
NEG_INF = -1e30


def rmsnorm(x, g):
    xf = x.astype(jnp.float32)
    y = xf * lax.rsqrt(jnp.mean(xf * xf, axis=-1, keepdims=True) + NORM_EPS)
    return (y * g.astype(jnp.float32)).astype(x.dtype)

def l2norm(x):
    return x * lax.rsqrt(jnp.sum(x * x, axis=-1, keepdims=True) + NORM_EPS)

def masked_softmax(s, mask):
    return jax.nn.softmax(jnp.where(mask, s, NEG_INF), axis=-1) * mask

def alibi_slopes_2(n):
    return jnp.asarray(2.0 ** (-8.0 * np.arange(1, n + 1) / n), jnp.float32)

def _chunks(x):
    b, t, h = x.shape[:3]
    x = x.reshape((b, t // CHUNK, CHUNK, h) + x.shape[3:])
    return jnp.moveaxis(x, 3, 1)

def _unchunk(o):
    n, b, h, c, d = o.shape
    return o.transpose(1, 0, 3, 2, 4).reshape(b, n * c, h, d)

def _causal_conv(x, w):
    return lax.conv_general_dilated(x, w[:, None, :], window_strides=(1,), padding=[(CONV_K - 1, 0)],
                                    dimension_numbers=('NWC', 'WIO', 'NWC'), feature_group_count=x.shape[-1])

def _hgrn2(q, f_logit, i, lb):
    b_, t_, h_, dk = q.shape
    dv = i.shape[-1]
    f = lb + (1.0 - lb) * jax.nn.sigmoid(f_logit)
    log_f = jnp.log(f)
    k = 1.0 - f
    xs = tuple(jnp.moveaxis(_chunks(a), 2, 0) for a in (q, k, i, log_f))
    tril = jnp.tril(jnp.ones((CHUNK, CHUNK), bool))[:, :, None]

    def step(S, inp):
        qn, kn, vn, ln = inp
        b = jnp.cumsum(ln, axis=2)
        decay = jnp.exp(jnp.where(tril, b[:, :, :, None, :] - b[:, :, None, :, :], -jnp.inf))
        intra = jnp.einsum('bhtd,bhsd,bhtsd->bhts', qn, kn, decay)
        o = jnp.einsum('bhts,bhse->bhte', intra, vn) + jnp.einsum('bhtd,bhde->bhte', qn * jnp.exp(b), S)
        b_end = b[:, :, -1:, :]
        S = jnp.exp(b_end[:, :, 0, :, None]) * S + jnp.einsum('bhsd,bhse->bhde', kn * jnp.exp(b_end - b), vn)
        return S, o

    S0 = jnp.zeros((b_, h_, dk, dv), jnp.float32)
    _, o = lax.scan(step, S0, xs)
    return _unchunk(o)

def _gated_delta(q, k, v, beta, log_decay):
    b_, t_, h_, dk = q.shape
    dv = v.shape[-1]
    qc, kc, vc = _chunks(q), _chunks(k), _chunks(v)
    bc = _chunks(beta)
    gc = jnp.cumsum(_chunks(log_decay), axis=-1)
    eye = jnp.eye(CHUNK, dtype=bool)
    tril = jnp.tril(jnp.ones((CHUNK, CHUNK), bool))
    decay = jnp.exp(jnp.where(tril, gc[..., :, None] - gc[..., None, :], -jnp.inf))
    kb = kc * bc[..., None]
    L = jnp.where(tril & ~eye, jnp.einsum('bhncd,bhnsd->bhncs', kb, kc) * decay, 0.0)
    rhs = jnp.concatenate([vc * bc[..., None], kb * jnp.exp(gc)[..., None]], axis=-1)
    sol = lax.linalg.triangular_solve(L + eye, rhs, left_side=True, lower=True, unit_diagonal=True)
    u, w = sol[..., :dv], sol[..., dv:]
    qk = jnp.einsum('bhncd,bhnsd->bhncs', qc, kc) * decay
    xs = tuple(jnp.moveaxis(a, 2, 0) for a in (qc, kc, u, w, qk, gc))

    def step(S, inp):
        qn, kn, un, wn, qkn, gn = inp
        v_new = un - jnp.einsum('bhcd,bhde->bhce', wn, S)
        o = (jnp.einsum('bhcd,bhde->bhce', qn * jnp.exp(gn)[..., None], S)
             + jnp.einsum('bhcs,bhse->bhce', qkn, v_new))
        g_end = gn[..., -1:]
        S = (jnp.exp(g_end)[..., None] * S
             + jnp.einsum('bhcd,bhce->bhde', kn * jnp.exp(g_end - gn)[..., None], v_new))
        return S, o

    S0 = jnp.zeros((b_, h_, dk, dv), jnp.float32)
    _, o = lax.scan(step, S0, xs)
    return _unchunk(o)

def _even_mixer(u, w_in, lb, conv_w, a_log, dt_bias, hgrn_g, gdn_g, w_out):
    b_, t_, _ = u.shape
    z = (u @ w_in).astype(jnp.float32)
    cuts = [int(c) for c in np.cumsum([A_QK, A_QK, A_WIDTH, A_WIDTH, B_QK, B_QK, B_WIDTH, B_WIDTH, B_HEADS])]
    aq, af, ai, ag, bq, bk, bv, bg, ba, bb = jnp.split(z, cuts, axis=-1)
    o_a = _hgrn2(aq.reshape(b_, t_, A_HEADS, A_DK), af.reshape(b_, t_, A_HEADS, A_DK),
                 ai.reshape(b_, t_, A_HEADS, A_DV), lb)
    o_a = rmsnorm(o_a, hgrn_g) * jax.nn.silu(ag.reshape(b_, t_, A_HEADS, A_DV))
    qkv = jax.nn.silu(_causal_conv(jnp.concatenate([bq, bk, bv], axis=-1), conv_w.astype(jnp.float32)))
    bq, bk, bv = jnp.split(qkv, [B_QK, 2 * B_QK], axis=-1)
    q = l2norm(bq.reshape(b_, t_, B_HEADS, B_DK)) * (B_DK ** -0.5)
    k = l2norm(bk.reshape(b_, t_, B_HEADS, B_DK))
    beta = jax.nn.sigmoid(bb)
    log_decay = -jnp.exp(a_log.astype(jnp.float32)) * jax.nn.softplus(ba + dt_bias.astype(jnp.float32))
    o_b = _gated_delta(q, k, bv.reshape(b_, t_, B_HEADS, B_DV), beta, log_decay)
    o_b = rmsnorm(o_b, gdn_g) * jax.nn.silu(bg.reshape(b_, t_, B_HEADS, B_DV))
    o = jnp.concatenate([o_a.reshape(b_, t_, A_WIDTH), o_b.reshape(b_, t_, B_WIDTH)], axis=-1)
    return o.astype(u.dtype) @ w_out

def _nsa_mixer(u, w_in, cmp_pos, cmp_w1, cmp_w2, w_out):
    b_, t_, _ = u.shape
    G, HP = C_GROUPS, C_HPG
    z = (u @ w_in).astype(jnp.float32)
    cuts = [C_Q + j * C_KV for j in range(7)]
    q, kc, vc, ks, vs, kw, vw, gl = jnp.split(z, cuts, axis=-1)
    kv = lambda a: a.reshape(b_, t_, G, C_DK)
    kc, vc, ks, vs, kw, vw = (kv(a) for a in (kc, vc, ks, vs, kw, vw))
    qg = q.reshape(b_, t_, G, HP, C_DK).transpose(0, 2, 3, 1, 4) * (C_DK ** -0.5)
    gates = jax.nn.sigmoid(gl.reshape(b_, t_, G, HP, 3)).transpose(0, 2, 3, 1, 4)
    slopes = alibi_slopes_2(C_HEADS).reshape(G, HP)
    tpos = jnp.arange(t_)

    n_cmp = (t_ - CMP_LEN) // CMP_STRIDE + 1
    cstart = jnp.arange(n_cmp) * CMP_STRIDE
    cidx = cstart[:, None] + jnp.arange(CMP_LEN)[None, :]

    def compress(a, pos, w1, w2):
        blk = a[:, cidx] + pos[None, None, :, None, :]
        blk = blk.transpose(0, 1, 3, 2, 4).reshape(b_, n_cmp, G, CMP_LEN * C_DK)
        return jax.nn.silu(blk @ w1) @ w2

    k_cmp = compress(kc, cmp_pos[0], cmp_w1[0], cmp_w2[0])
    v_cmp = compress(vc, cmp_pos[1], cmp_w1[1], cmp_w2[1])
    dist_c = tpos[:, None] - (cstart + CMP_LEN - 1)[None, :]
    s_c = jnp.einsum('bghtd,bjgd->bghtj', qg, k_cmp) - slopes[:, :, None, None] * dist_c
    p_c = masked_softmax(s_c, dist_c >= 0)
    o_cmp = jnp.einsum('bghtj,bjge->bghte', p_c, v_cmp)

    n_blk = t_ // SEL_BLOCK
    n_sel = min(N_SEL, n_blk)
    bstart = jnp.arange(n_blk) * SEL_BLOCK
    overlap = ((cstart[:, None] < bstart[None, :] + SEL_BLOCK)
               & (cstart[:, None] + CMP_LEN > bstart[None, :])).astype(jnp.float32)
    imp = jnp.einsum('bghtj,ji->bgti', p_c, overlap)
    cur = (tpos // SEL_BLOCK)[:, None]
    bi = jnp.arange(n_blk)[None, :]
    forced = (bi == 0) | (bi == cur) | (bi == cur - 1)
    score = jnp.where(forced, SEL_FORCE, jnp.where(bi > cur, -SEL_FORCE, imp))
    _, sel_idx = lax.top_k(score, n_sel)

    ks_blocks = ks.reshape(b_, n_blk, SEL_BLOCK, G, C_DK).transpose(0, 3, 1, 2, 4)
    vs_blocks = vs.reshape(b_, n_blk, SEL_BLOCK, G, C_DV).transpose(0, 3, 1, 2, 4)
    nqb = t_ // SEL_Q_BLOCK
    q_b = qg.reshape(b_, G, HP, nqb, SEL_Q_BLOCK, C_DK).transpose(3, 0, 1, 2, 4, 5)
    idx_b = sel_idx.reshape(b_, G, nqb, SEL_Q_BLOCK, n_sel).transpose(2, 0, 1, 3, 4)
    t_b = tpos.reshape(nqb, SEL_Q_BLOCK)
    gather = jax.vmap(jax.vmap(lambda blocks, ix: blocks[ix]))
    n_keys = n_sel * SEL_BLOCK

    def sel_block(args):
        qb, ib, tb = args
        kg = gather(ks_blocks, ib).reshape(b_, G, SEL_Q_BLOCK, n_keys, C_DK)
        vg = gather(vs_blocks, ib).reshape(b_, G, SEL_Q_BLOCK, n_keys, C_DV)
        kpos = (ib[..., None] * SEL_BLOCK + jnp.arange(SEL_BLOCK)).reshape(b_, G, SEL_Q_BLOCK, n_keys)
        dist = tb[None, None, :, None] - kpos
        s = (jnp.einsum('bghqd,bgqkd->bghqk', qb, kg)
             - slopes[None, :, :, None, None] * dist[:, :, None])
        p = masked_softmax(s, (dist >= 0)[:, :, None])
        return jnp.einsum('bghqk,bgqke->bghqe', p, vg)

    o_slc = lax.map(sel_block, (q_b, idx_b, t_b))
    o_slc = o_slc.transpose(1, 2, 3, 0, 4, 5).reshape(b_, G, HP, t_, C_DV)

    nwb = t_ // Q_BLOCK
    band = jnp.arange(nwb)[:, None] * Q_BLOCK + jnp.arange(Q_BLOCK + WINDOW)[None, :]
    pad = ((0, 0), (0, 0), (WINDOW, 0), (0, 0))
    kb = jnp.pad(kw.transpose(0, 2, 1, 3), pad)[:, :, band]
    vb = jnp.pad(vw.transpose(0, 2, 1, 3), pad)[:, :, band]
    kpos = band - WINDOW
    dist_w = tpos.reshape(nwb, Q_BLOCK)[:, :, None] - kpos[:, None, :]
    valid_w = (dist_w >= 0) & (dist_w < WINDOW) & (kpos[:, None, :] >= 0)
    qw = qg.reshape(b_, G, HP, nwb, Q_BLOCK, C_DK)
    s_w = jnp.einsum('bghnqd,bgnkd->bghnqk', qw, kb) - slopes[:, :, None, None, None] * dist_w
    p_w = masked_softmax(s_w, valid_w)
    o_win = jnp.einsum('bghnqk,bgnke->bghnqe', p_w, vb).reshape(b_, G, HP, t_, C_DV)

    o = gates[..., 0:1] * o_cmp + gates[..., 1:2] * o_slc + gates[..., 2:3] * o_win
    o = o.transpose(0, 3, 1, 2, 4).reshape(b_, t_, ODD_OUT_2)
    return o.astype(u.dtype) @ w_out

def _swiglu(u, w_gu, w_down):
    gate, up = jnp.split(u @ w_gu, 2, axis=-1)
    return (jax.nn.silu(gate) * up) @ w_down

def second_inputs(seed: int = 0) -> dict:
    key = jax.random.key(seed)
    ks = jax.random.split(key, 20)
    f32 = jnp.float32
    nrm = lambda k, shape: jax.random.normal(k, shape, f32)
    w = lambda k, shape, fan_in: nrm(k, shape) * fan_in ** -0.5
    dt = jnp.exp(jax.random.uniform(ks[6], (N_EVEN, B_HEADS), f32, np.log(1e-3), np.log(1e-1)))
    return {
        'x': nrm(ks[0], (BATCH, SEQ, D_MODEL)),
        'norm_g': 1.0 + 0.05 * nrm(ks[1], (DEPTH, 4, D_MODEL)),
        'ab_w_in': w(ks[2], (N_EVEN, D_MODEL, EVEN_IN_2), D_MODEL),
        'hgrn_lb_logits': 0.5 * nrm(ks[3], (N_EVEN, A_QK)),
        'gdn_conv_w': w(ks[4], (N_EVEN, CONV_K, 2 * B_QK + B_WIDTH), CONV_K),
        'gdn_a_log': jnp.log(jax.random.uniform(ks[5], (N_EVEN, B_HEADS), f32, 1.0, 16.0)),
        'gdn_dt_bias': dt + jnp.log(-jnp.expm1(-dt)),
        'hgrn_norm_g': 1.0 + 0.05 * nrm(ks[7], (N_EVEN, A_DV)),
        'gdn_norm_g': 1.0 + 0.05 * nrm(ks[8], (N_EVEN, B_DV)),
        'ab_w_out': w(ks[9], (N_EVEN, EVEN_OUT_2, D_MODEL), EVEN_OUT_2),
        'nsa_w_in': w(ks[10], (N_ODD, D_MODEL, ODD_IN_2), D_MODEL),
        'nsa_cmp_pos': 0.1 * nrm(ks[11], (N_ODD, 2, CMP_LEN, C_DK)),
        'nsa_cmp_w1': w(ks[12], (N_ODD, 2, CMP_LEN * C_DK, C_DK), CMP_LEN * C_DK),
        'nsa_cmp_w2': w(ks[13], (N_ODD, 2, C_DK, C_DK), C_DK),
        'nsa_w_out': w(ks[14], (N_ODD, ODD_OUT_2, D_MODEL), ODD_OUT_2),
        'ffn_w_gu': w(ks[15], (DEPTH, D_MODEL, 2 * D_FF), D_MODEL),
        'ffn_w_down': w(ks[16], (DEPTH, D_FF, D_MODEL), D_FF),
    }

def second_block(x, norm_g, ab_w_in, hgrn_lb_logits, gdn_conv_w, gdn_a_log, gdn_dt_bias, hgrn_norm_g,
              gdn_norm_g, ab_w_out, nsa_w_in, nsa_cmp_pos, nsa_cmp_w1, nsa_cmp_w2, nsa_w_out,
              ffn_w_gu, ffn_w_down):
    lb_all = jnp.cumsum(jax.nn.softmax(hgrn_lb_logits.astype(jnp.float32), axis=0), axis=0)
    lb_all = lb_all - lb_all[:1]
    h = x
    for layer in range(DEPTH):
        j = layer // 2
        u = rmsnorm(h, norm_g[layer, 0])
        if layer % 2 == 0:
            m = _even_mixer(u, ab_w_in[j], lb_all[j].reshape(A_HEADS, A_DK), gdn_conv_w[j], gdn_a_log[j],
                            gdn_dt_bias[j], hgrn_norm_g[j], gdn_norm_g[j], ab_w_out[j])
        else:
            m = _nsa_mixer(u, nsa_w_in[j], nsa_cmp_pos[j], nsa_cmp_w1[j], nsa_cmp_w2[j], nsa_w_out[j])
        h = h + rmsnorm(m, norm_g[layer, 1])
        u = rmsnorm(h, norm_g[layer, 2])
        h = h + rmsnorm(_swiglu(u, ffn_w_gu[layer], ffn_w_down[layer]), norm_g[layer, 3])
    return h


def setup_inputs(seed=0):
    out = dict(first_inputs(seed))
    for name, value in second_inputs(seed + 1).items():
        if name != "x":
            out[name + "_2"] = value
    return out


def reference(
    x, ev_norm, ev_w_in, ev_conv_w, ev_conv_b, ev_w_a, ev_b_a, ev_w_i, ev_b_i, ev_lam, ev_w_out,
    od_norm, od_w_in, od_w_alpha, od_b_alpha, od_head_norm, od_v_norm, od_w_s, od_b_s, od_w_out,
    final_norm, norm_g_2, ab_w_in_2, hgrn_lb_logits_2, gdn_conv_w_2, gdn_a_log_2, gdn_dt_bias_2,
    hgrn_norm_g_2, gdn_norm_g_2, ab_w_out_2, nsa_w_in_2, nsa_cmp_pos_2, nsa_cmp_w1_2,
    nsa_cmp_w2_2, nsa_w_out_2, ffn_w_gu_2, ffn_w_down_2,
):
    x = first_block(
        x, ev_norm, ev_w_in, ev_conv_w, ev_conv_b, ev_w_a, ev_b_a, ev_w_i, ev_b_i, ev_lam,
        ev_w_out, od_norm, od_w_in, od_w_alpha, od_b_alpha, od_head_norm, od_v_norm, od_w_s,
        od_b_s, od_w_out, final_norm,
    )
    return second_block(
        x, norm_g_2, ab_w_in_2, hgrn_lb_logits_2, gdn_conv_w_2, gdn_a_log_2, gdn_dt_bias_2,
        hgrn_norm_g_2, gdn_norm_g_2, ab_w_out_2, nsa_w_in_2, nsa_cmp_pos_2, nsa_cmp_w1_2,
        nsa_cmp_w2_2, nsa_w_out_2, ffn_w_gu_2, ffn_w_down_2,
    )


_drawn_inputs = setup_inputs


def setup_inputs(seed=0):
    import zlib

    import numpy as np

    out = dict(_drawn_inputs(seed))
    spreads = {}
    factors = {'hgrn_norm_g_2': 8.0, 'gdn_norm_g_2': 8.0, 'nsa_cmp_pos_2': 6.089}
    for name, (base, spread) in spreads.items():
        noise = np.random.default_rng([zlib.crc32(name.encode()), seed]).standard_normal(out[name].shape)
        drawn = base * np.exp(spread * noise) if base else spread * noise
        out[name] = __import__('jax').numpy.asarray(drawn.astype(out[name].dtype))
    for name, factor in factors.items():
        out[name] = (out[name] * factor).astype(out[name].dtype)
    return out
```

```python
from contextlib import ExitStack

import numpy as np

import concourse.bass as bass
from concourse import mybir

F32 = mybir.dt.float32
F32R = mybir.dt.float32r
I32 = mybir.dt.int32
ALU = mybir.AluOpType
ACT = mybir.ActivationFunctionType
AX = mybir.AxisListType
MUL, ADD, SUB, MAX, MIN = ALU.mult, ALU.add, ALU.subtract, ALU.max, ALU.min

D = 2048
EPS = 1e-6
SQ = 128.0 ** -0.5
NRAW = 4
TILE = 2048

C_ID = 0
C_ZERO = 128
C_TRI = 256
C_ONE = 384
C_LEV = 512
C_EPS = C_LEV + 7 * 128
C_N = C_EPS + 1

COLS = [("ev_norm", 16), ("ev_conv_w", 48), ("ev_conv_b", 12), ("ev_b_a", 12), ("ev_b_i", 12), ("ev_lam", 12),
        ("od_norm", 16), ("od_b_alpha", 4), ("od_b_s", 4), ("norm00", 16), ("norm02", 16), ("norm10", 16),
        ("norm12", 16), ("gdn_conv", 96), ("lb", 8), ("a_log", 8), ("dt_bias", 8), ("pos0", 32), ("pos1", 32)]
COL_AT = {}
_n = 0
for _k, _w in COLS:
    COL_AT[_k] = (_n, _w)
    _n += _w
COL_N = _n

M_G = [0, 384, 768]
M_C = 1152
M_CMP = 1536
M_VAL = M_CMP + 32
M_N = M_VAL + 32

SLOPE = [[2.0 ** (-8.0 * (g + 3 * j + 1) / 12) for j in range(4)] for g in range(3)]
SLOPE2 = [2.0 ** (-8.0 * (h + 1) / 16) for h in range(16)]


def constants():
    s = np.arange(128)[:, None]
    t = np.arange(128)[None, :]
    parts = [np.eye(128), np.zeros((128, 128)), s <= t, np.ones((128, 128))]
    for level in range(7):
        h = 1 << level
        parts.append((s // (2 * h) == t // (2 * h)) & (s % (2 * h) < h) & (t % (2 * h) >= h))
    parts.append(np.full((128, 1), EPS))
    return np.concatenate([np.asarray(x, np.float32) for x in parts], axis=1)


def distances():
    out = []
    big = 1e32
    for dil, most in ((1, 128), (4, 512), (16, 2048), (1, 512)):
        for base, n in ((0, 128), (128, 256)):
            d = base + np.arange(128)[:, None] - np.arange(n)[None, :]
            ok = (d >= 0) & (d <= most) & (d % dil == 0)
            out.append(np.where(ok, d, big))
    for keep in (False, True):
        for base in (0, 128):
            d = base + np.arange(128)[:, None] - (16 * np.arange(15)[None, :] + 31)
            v = (d >= 0) if keep else np.where(d >= 0, d, big)
            out += [v, np.zeros((128, 1))]
    return np.concatenate([np.asarray(x, np.float32) for x in out], axis=1)


class Engine:

    def __init__(self, sem):
        self.sem = sem
        self.list = []
        self.n = 0
        self.past = {}

    def wait(self, *toks):
        for t in toks:
            if t is None:
                continue
            if isinstance(t, list):
                self.wait(*t)
                continue
            sem, v = t
            if self.past.get(id(sem), 0) < v:
                self.past[id(sem)] = v
                self.list.append(lambda e, sem=sem, v=v: e.wait_ge(sem, v))

    def do(self, fn, *toks, sig=True):
        self.wait(*toks)
        if not sig:
            self.list.append(fn)
            return None
        self.n += 1
        self.list.append(lambda e: fn(e).then_inc(self.sem, 1))
        return (self.sem, self.n)

    def now(self):
        return (self.sem, self.n)

    def dma(self, out, in_, sem, *toks):
        self.wait(*toks)
        self.list.append(lambda e: e.dma_start(out, in_).then_inc(sem[0], 16))
        sem[1] += 16
        return (sem[0], sem[1])

    def tt(self, out, a, b, op, *w):
        return self.do(lambda e: e.tensor_tensor(out, a, b, op), *w)

    def ts(self, out, a, s1, s2, op0, op1, *w):
        if op1 is None:
            return self.do(lambda e: e.tensor_scalar(out, a, s1, None, op0), *w)
        return self.do(lambda e: e.tensor_scalar(out, a, s1, s2, op0, op1), *w)

    def stt(self, out, a, s, b, op0, op1, *w):
        return self.do(lambda e: e.scalar_tensor_tensor(out=out, in0=a, scalar=s, in1=b, op0=op0, op1=op1), *w)

    def cp(self, out, a, *w):
        return self.do(lambda e: e.tensor_copy(out, a), *w)

    def rec(self, out, a, *w):
        return self.do(lambda e: e.reciprocal(out, a), *w)

    def red(self, out, a, op, *w):
        return self.do(lambda e: e.tensor_reduce(out, a, AX.X, op), *w)

    def pred(self, out, mask, a, *w):
        return self.do(lambda e: e.copy_predicated(out, mask, a), *w)

    def act(self, out, a, func, *w, bias=None, scale=None, acc=None):
        kw = {}
        if bias is not None:
            kw["bias"] = bias
        if scale is not None:
            kw["scale"] = scale
        if acc is not None:
            kw["accum_out"] = acc
        return self.do(lambda e: e.activation(out, a, func, **kw), *w)

    def mm(self, out, l, r, *w, start=True, stop=True, sig=False):
        return self.do(lambda e: e.matmul(out, l, r, start=start, stop=stop, skip_group_check=True), *w, sig=sig)

    def tr(self, out, a, ident, *w, sig=False):
        return self.do(lambda e: e.transpose(out, a, ident), *w, sig=sig)


class Slot:
    def __init__(self, t):
        self.t = t
        self.free = []
        self.held = False

    def done(self, *toks):
        assert self.held
        self.free = list(toks)
        self.held = False


class Ring:

    def __init__(self, items):
        self.slots = [Slot(x) for x in items]
        self.i = 0

    def get(self):
        s = self.slots[self.i % len(self.slots)]
        self.i += 1
        assert not s.held
        s.held = True
        return s


def skew(n, stages):
    m = len(stages)
    for t in range(n + m - 1):
        for s in reversed(range(m)):
            if 0 <= t - s < n:
                stages[s](t - s)


def bc(ap, shape):
    return ap.to_broadcast(shape)


class Program:
    def __init__(self, nc, ctx):
        self.nc = nc
        self.ctx = ctx
        sem = lambda n: ctx.enter_context(nc.semaphore(n))
        self.sem = sem
        self.V, self.A, self.P, self.G, self.S = (Engine(sem("s_" + n)) for n in ("dve", "act", "pe", "pool", "sp"))
        self.ws = [[sem(f"s_w{i}"), 0] for i in range(NRAW)]
        self.ls = {}
        sb = self.sb
        self.raw = Ring([sb(f"raw{i}", [128, TILE])[:, :] for i in range(NRAW)])
        self.hi = Ring([sb(f"whi{i}", [128, TILE], F32R)[:, :] for i in range(2)])
        self.lo = Ring([sb(f"wlo{i}", [128, TILE], F32R)[:, :] for i in range(2)])
        self.x = sb("xres", [128, 2, D])
        self.xhi = sb("xhi", [128, 16, 256], F32R)
        self.xlo = sb("xlo", [128, 16, 256], F32R)
        self.cst = sb("cst", [128, C_N])
        self.col = sb("col", [128, COL_N])
        self.st = sb("st", [128, 512])
        self.st_i = 0
        self.ps = Ring([ctx.enter_context(nc.psum_tensor(f"ps{i}", [128, 512], F32))[:, :] for i in range(8)])
        self.ident = self.cst[:, C_ID:C_ID + 128]
        self.x_t = []

    def sb(self, name, shape, dt=F32, ctx=None):
        return (ctx or self.ctx).enter_context(self.nc.sbuf_tensor(name, shape, dt))

    def load(self, name, out, in_, *w, eng=None):
        if name not in self.ls:
            self.ls[name] = [self.sem("s_l_" + name), 0]
        return (eng or self.G).dma(out, in_, self.ls[name], *w)

    def c(self, name, i=0, n=1):
        a, w = COL_AT[name]
        return self.col[:, a + i:a + i + n]

    def cell(self, n=1):
        if self.st_i + n > 512:
            self.st_i = 0
        a = self.st_i
        self.st_i += n
        return self.st[:, a:a + n]

    def barrier(self):
        now = [e.now() for e in (self.V, self.A, self.P, self.G)]
        for e in (self.V, self.A, self.P, self.G):
            e.wait(now)
        return now

    def tile(self, src, n=TILE):
        s = self.raw.get()
        k = (self.raw.i - 1) % NRAW
        tok = self.S.dma(s.t[:, 0:n], src, self.ws[k], s.free)
        return s, tok

    def split(self, src, n=TILE):
        s, tok = self.tile(src, n)
        h, l = self.hi.get(), self.lo.get()
        th = self.A.act(h.t[:, 0:n], s.t[:, 0:n], ACT.Copy, tok, h.free)
        tl = self.V.tt(l.t[:, 0:n], s.t[:, 0:n], h.t[:, 0:n].bitcast(F32), SUB, tok, th, l.free)
        s.done(th, tl)
        return h, l, tl

    def proj(self, src, tiles, mode, lhs=None, lt=None, koff=0):
        V, A, P = self.V, self.A, self.P
        xhi, xlo = lhs or (self.xhi, self.xlo)
        b = [self.ps.get(), self.ps.get()]
        n = len(tiles)
        P.wait(lt)
        for i, ti in enumerate(tiles):
            h, l, tok = self.split(src[ti])
            P.wait(tok)
            if i == 0:
                P.wait(b[0].free, b[1].free)
            for j in range(4):
                k = koff + 4 * i + j
                first, last = i == 0 and j == 0, i == n - 1 and j == 3
                if mode == "A":
                    wh, wl = h.t[:, j * 512:(j + 1) * 512], l.t[:, j * 512:(j + 1) * 512]
                    for tt in range(2):
                        a, c = xhi[:, k, tt * 128:(tt + 1) * 128], xlo[:, k, tt * 128:(tt + 1) * 128]
                        P.mm(b[tt].t, a, wh, start=first, stop=False)
                        P.mm(b[tt].t, a, wl, start=False, stop=False)
                        t = P.mm(b[tt].t, c, wh, start=False, stop=last, sig=(j == 3 and tt == 1))
                else:
                    for f in range(4):
                        o = j * 512 + f * 128
                        out = b[f // 2].t[:, (f % 2) * 256:(f % 2) * 256 + 256]
                        P.mm(out, h.t[:, o:o + 128], xhi[:, k, :], start=first and f % 2 == 0, stop=False)
                        P.mm(out, h.t[:, o:o + 128], xlo[:, k, :], start=False, stop=False)
                        t = P.mm(out, l.t[:, o:o + 128], xhi[:, k, :], start=False, stop=last,
                                 sig=(j == 3 and f == 3))
            h.done(t)
            l.done(t)
        return b, t

    def proj_small(self, src, nc_, lt=None):
        P = self.P
        h, l, tok = self.split(src, 16 * nc_)
        b = self.ps.get()
        P.wait(tok, b.free, lt)
        for tt in range(2):
            out = b.t[:, tt * 64:tt * 64 + nc_]
            for k in range(16):
                a, c = self.xhi[:, k, tt * 128:(tt + 1) * 128], self.xlo[:, k, tt * 128:(tt + 1) * 128]
                wh, wl = h.t[:, k * nc_:(k + 1) * nc_], l.t[:, k * nc_:(k + 1) * nc_]
                P.mm(out, a, wh, start=(tt == 0 and k == 0), stop=False)
                P.mm(out, a, wl, start=False, stop=False)
                t = P.mm(out, c, wh, start=False, stop=(k == 15), sig=(k == 15))
        h.done(t)
        l.done(t)
        return b, t

    def rsqrt(self, ss, n, scale, *w):
        V, A = self.V, self.A
        v, r, a = self.cell(n), self.cell(n), self.cell(n)
        t1 = V.ts(v, ss, scale, EPS, MUL, ADD, *w)
        t2 = A.act(a, v, ACT.Ln, t1)
        t3 = A.act(r, a, ACT.Exp, t2, scale=-0.5)
        t4 = V.tt(a, r, r, MUL, t3)
        t5 = V.tt(a, a, v, MUL, t4)
        t6 = V.ts(a, a, -0.5, 1.5, MUL, ADD, t5)
        t7 = V.tt(r, r, a, MUL, t6)
        return r, t7

    def row_rstd(self, x, junk, tt, *w):
        ss = self.cell()
        t = self.A.act(junk, x, ACT.Square, *w, acc=ss)
        return self.rsqrt(ss, 1, 1.0 / D, t)

    def norm_T(self, xn, gname, xt):
        V, A, P = self.V, self.A, self.P
        tn = []
        for tt in range(2):
            r, t = self.row_rstd(self.x[:, tt, :], xn[:, tt, :], tt, xt)
            tn.append(V.ts(xn[:, tt, :], self.x[:, tt, :], r, None, MUL, None, t))
        out = []
        for c in range(0, 16, 2):
            b = self.ps.get()
            P.wait(b.free, tn)
            for i in range(2):
                for tt in range(2):
                    t = P.tr(b.t[:, i * 256 + tt * 128:i * 256 + tt * 128 + 128],
                             xn[:, tt, (c + i) * 128:(c + i + 1) * 128], self.ident, sig=True)
            for i in range(2):
                th = A.act(self.xhi[:, c + i, :], b.t[:, i * 256:(i + 1) * 256], ACT.Copy, t,
                           scale=self.c(gname, c + i))
            for i in range(2):
                tl = V.stt(self.xlo[:, c + i, :], b.t[:, i * 256:(i + 1) * 256], self.c(gname, c + i),
                           self.xhi[:, c + i, :].bitcast(F32), MUL, SUB, th)
            b.done(tl)
            out = [th, tl]
        return out

    def to_lhs(self, src, c, n, *w):
        th = self.A.act(self.xhi[:, c:c + n, :], src, ACT.Copy, *w)
        tl = self.V.tt(self.xlo[:, c:c + n, :], src, self.xhi[:, c:c + n, :].bitcast(F32), SUB, *w, th)
        return [th, tl]

    def turn(self, src, c0, nch, *w):
        P = self.P
        for c in range(0, nch, 2):
            b = self.ps.get()
            P.wait(b.free, *w)
            for i in range(2):
                for tt in range(2):
                    t = P.tr(b.t[:, i * 256 + tt * 128:i * 256 + tt * 128 + 128],
                             src[:, tt, (c + i) * 128:(c + i + 1) * 128], self.ident, sig=True)
            o = self.xhi[:, c0 + c:c0 + c + 2, :]
            p = b.t.rearrange("p (c n) -> p c n", c=2)
            th = self.A.act(o, p, ACT.Copy, t)
            tl = self.V.tt(self.xlo[:, c0 + c:c0 + c + 2, :], p, o.bitcast(F32), SUB, th)
            b.done(tl)
        return [th, tl]

    def out_residual(self, src, lt):
        for nb in range(4):
            b, t = self.proj(src, range(nb * 4, nb * 4 + 4), "A", lt=lt)
            for tt in range(2):
                xs = self.x[:, tt, nb * 512:(nb + 1) * 512]
                tv = self.V.tt(xs, b[tt].t, xs, ADD, t)
                b[tt].done(tv)
        return tv

    def out_post(self, src, lt, m, gbc, gt):
        for nb in range(4):
            b, t = self.proj(src, range(nb * 4, nb * 4 + 4), "A", lt=lt)
            for tt in range(2):
                ta = self.A.act(m[:, tt, nb * 512:(nb + 1) * 512], b[tt].t, ACT.Copy, t)
                b[tt].done(ta)
        return self.post(m, gbc, ta, gt)

    def post(self, m, gbc, mt, gt):
        out = []
        for tt in range(2):
            xs = self.x[:, tt, :]
            r, t = self.row_rstd(m[:, tt, :], self.junk[:, :], tt, mt)
            t1 = self.V.stt(m[:, tt, :], m[:, tt, :], r, gbc, MUL, MUL, t, gt)
            out = [self.V.tt(xs, xs, m[:, tt, :], ADD, t1)]
        return out

    def headnorm(self, o, nh, dv, gb, gate, *w):
        V, A = self.V, self.A
        sq = self.junk
        out = []
        for tt in range(2):
            oo = o[:, tt, :].rearrange("p (h e) -> p h e", h=nh)
            s3 = sq[:, 0:nh * dv].rearrange("p (h e) -> p h e", h=nh)
            t1 = A.act(sq[:, 0:nh * dv], o[:, tt, :], ACT.Square, *w, self.V.now())
            ss = self.cell(nh)
            t2 = V.red(ss, s3, ADD, t1)
            r, t3 = self.rsqrt(ss, nh, 1.0 / dv, t2)
            t4 = V.tt(oo, oo, bc(r.unsqueeze(2), [128, nh, dv]), MUL, t3)
            g = gb if gb.shape[1] == nh * dv else None
            if g is None:
                t5 = V.tt(oo, oo, bc(gb.unsqueeze(1), [128, nh, dv]), MUL, t4)
            else:
                t5 = V.tt(o[:, tt, :], o[:, tt, :], g, MUL, t4)
            out.append(V.tt(o[:, tt, :], o[:, tt, :], gate[:, tt, :], MUL, t5))
        return out

    def ffn(self, a, layer, tag):
        V, A, P = self.V, self.A, self.P
        with ExitStack() as c:
            hh = self.sb("hh" + tag, [128, 24, 256], F32R, c)
            hl = self.sb("hl" + tag, [128, 24, 256], F32R, c)
            m = self.sb("fm" + tag, [128, 2, D], F32, c)
            gbc = self.sb("fg" + tag, [128, D], F32, c)
            tmp = Ring([self.sb(f"ft{tag}{i}", [128, 512], F32, c)[:, :] for i in range(2)])
            self.junk = self.sb("fj" + tag, [128, D], F32, c)
            bt = self.barrier()
            gt = self.load("gbc", gbc[:, :], a[f"g_post{layer}3"], bt)
            lt = self.norm_T(m, f"norm{layer}2", self.x_t)
            wgu, wd = a["ffn_gu"][layer], a["ffn_down"][layer]
            done = None
            for half, blocks in enumerate((range(0, 6), range(6, 11))):
                for i, nb in enumerate(blocks):
                    bg, tg = self.proj(wgu, range(nb * 4, nb * 4 + 4), "B", lt=lt)
                    sg = []
                    for q in range(2):
                        s = tmp.get()
                        t1 = A.act(s.t, bg[q].t, ACT.Silu, tg, s.free)
                        bg[q].done(t1)
                        sg.append((s, t1))
                    bu, tu = self.proj(wgu, range((11 + nb) * 4, (11 + nb) * 4 + 4), "B", lt=lt)
                    for q in range(2):
                        s, t1 = sg[q]
                        t2 = V.tt(s.t, s.t, bu[q].t, MUL, tu, t1)
                        bu[q].done(t2)
                        k = i * 4 + q * 2
                        s3 = s.t.rearrange("p (c n) -> p c n", c=2)
                        t3 = A.act(hh[:, k:k + 2, :], s3, ACT.Copy, t2, done)
                        t4 = V.tt(hl[:, k:k + 2, :], s3, hh[:, k:k + 2, :].bitcast(F32), SUB, t3, done)
                        s.done(t3, t4)
                n = len(blocks)
                for nb in range(4):
                    b, t = self.proj(wd, range(nb * 11 + half * 6, nb * 11 + half * 6 + n), "A", (hh, hl), [t3, t4])
                    for tt in range(2):
                        ms = m[:, tt, nb * 512:(nb + 1) * 512]
                        if half == 0:
                            tm = A.act(ms, b[tt].t, ACT.Copy, t, V.now())
                        else:
                            tm = V.tt(ms, ms, b[tt].t, ADD, t, A.now())
                        b[tt].done(tm)
                done = [t, tm]
            self.x_t = self.post(m, gbc[:, :], tm, gt)

    def decay_attention(self, q, k, b, v, o, nh, dv, E, At, Ac, rt, o_from=None):
        V, A, P = self.V, self.A, self.P
        nI = nh * 2
        lev = lambda l: self.cst[:, C_LEV + l * 128:C_LEV + (l + 1) * 128]
        t0 = V.do(lambda e: e.memset(At[:, :], 0.0), rt)
        ring = Ring(E)

        def inst(ap, i):
            return ap[:, (i // 2) * 256 + (i % 2) * 128:(i // 2) * 256 + (i % 2) * 128 + 128]

        def masks(m, lhs, rhs, w, rel):
            for g in range(0, nI, 4):
                bk = self.ps.get()
                P.wait(bk.free, w)
                for i in range(4):
                    t = P.mm(bk.t[:, i * 128:(i + 1) * 128], inst(lhs, g + i), inst(rhs, g + i),
                             start=(i == 0), stop=True, sig=True)
                tv = V.pred(At[:, g * 128:(g + 4) * 128].rearrange("p (i t) -> p i t", i=4),
                            bc(m.bitcast(I32).unsqueeze(1), [128, 4, 128]),
                            bk.t.rearrange("p (i t) -> p i t", i=4), t, t0)
                bk.done(tv)
            return t

        masks(self.ident, k, q, rt, None)
        for level in range(8):
            h = 1 << level
            sl = ring.get()
            X = sl.t
            r3 = lambda ap: ap.rearrange("p (m n) -> p m n", n=2 * h)
            B, K, Q, X3 = r3(b), r3(k), r3(q), r3(X)
            m = nh * 256 // (2 * h)
            ref = bc(B[:, :, h - 1:h], [128, m, h])
            t1 = V.tt(X3[:, :, 0:h], ref, B[:, :, 0:h], SUB, rt, sl.free)
            t2 = V.tt(X3[:, :, h:2 * h], B[:, :, h:2 * h], ref, SUB, rt, sl.free)
            t3 = A.act(X, X, ACT.Exp, t1, t2)
            t4 = V.tt(X3[:, :, 0:h], X3[:, :, 0:h], K[:, :, 0:h], MUL, t3)
            t5 = V.tt(X3[:, :, h:2 * h], X3[:, :, h:2 * h], Q[:, :, h:2 * h], MUL, t3)
            if level < 7:
                sl.done(masks(lev(level), X, X, [t4, t5], None))
            else:
                for g in range(0, nh, 4):
                    bk = self.ps.get()
                    P.wait(bk.free, t4, t5)
                    for i in range(4):
                        hd = g + i
                        t = P.mm(bk.t[:, i * 128:(i + 1) * 128], X[:, hd * 256:hd * 256 + 128],
                                 X[:, hd * 256 + 128:hd * 256 + 256], start=(i == 0), stop=True, sig=True)
                    tc = A.act(Ac[:, g * 128:(g + 4) * 128], bk.t, ACT.Copy, t)
                    bk.done(tc)
        ta = V.now()
        per = 512 // dv
        for tt in range(2):
            for g in range(0, nh, per):
                bk = self.ps.get()
                P.wait(bk.free, ta, tc)
                for i in range(per):
                    hd = g + i
                    out = bk.t[:, i * dv:(i + 1) * dv]
                    vv = lambda x: v[:, x, hd * dv:(hd + 1) * dv]
                    a = inst_at(At, hd * 2 + tt)
                    t = P.mm(out, a, vv(tt), start=(i == 0), stop=(tt == 0), sig=True)
                    if tt == 1:
                        t = P.mm(out, Ac[:, hd * 128:(hd + 1) * 128], vv(0), start=False, stop=True, sig=True)
                to = A.act(o[:, tt, g * dv:(g + per) * dv], bk.t, ACT.Copy, t, o_from)
                bk.done(to)
        return to


def inst_at(ap, i):
    return ap[:, i * 128:(i + 1) * 128]


def layer1(p, a):
    V, A, P, G = p.V, p.A, p.P, p.G
    with ExitStack() as c:
        sb = lambda n, s: p.sb("l1" + n, s, F32, c)
        xa = sb("xa", [128, 12, 260])
        xc = sb("xc", [128, 12, 256])
        R = sb("r", [128, 12, 256])
        I = sb("i", [128, 12, 256])
        ga = sb("ga", [128, 12, 256])
        vt = sb("vt", [128, 2, 1536])
        gb = sb("gb", [128, 4, 256])
        dm = xa[:, :, :].rearrange("p c n -> p (c n)")
        xn = vt[:, :, :].rearrange("p a n -> p (a n)")
        p.barrier()
        big = sb("mb", [128, 1024])
        xn = ga[:, :, :].rearrange("p c n -> p (c n)")
        rn = R[:, :, :].rearrange("p c n -> p (c n)")
        inn = I[:, :, :].rearrange("p c n -> p (c n)")
        xnv = [rn[:, 0:D], inn[:, 0:D]]

        class XN:
            def __getitem__(self, k):
                return xnv[k[1]][:, k[2]]

        lt = p.norm_T(XN(), "ev_norm", p.x_t)
        tz = V.do(lambda e: e.memset(xa[:, :, 0:3], 0.0))
        w = a["ev_in"]
        tx = None
        for nb in range(3):
            b, t = p.proj(w, range(nb * 4, nb * 4 + 4), "B", lt=lt)
            for q in range(2):
                k = nb * 4 + q * 2
                tx = A.act(xa[:, k:k + 2, 3:259], b[q].t.rearrange("p (c n) -> p c n", c=2), ACT.Copy, t)
                b[q].done(tx)
        lam = p.c("ev_lam", 0, 12)
        c8, s1, s2 = p.cell(12), p.cell(12), p.cell(12)
        t1 = V.stt(s1, lam, -1.0, lam, MUL, MAX, p.cst_t)
        t2 = A.act(s1, s1, ACT.Exp, t1, scale=-1.0)
        t3 = A.act(s1, s1, ACT.Ln, t2, bias=1.0)
        t4 = V.ts(s2, lam, -1.0, 0.0, MUL, MAX, t1)
        t5 = V.tt(s2, s1, s2, ADD, t3, t4)
        tc8 = V.ts(c8, s2, -8.0, None, MUL, None, t5)
        for nb in range(3):
            b, t = p.proj(w, range((3 + nb) * 4, (3 + nb) * 4 + 4), "B")
            for q in range(2):
                k = nb * 4 + q * 2
                tga = A.act(ga[:, k:k + 2, :], b[q].t.rearrange("p (c n) -> p c n", c=2), ACT.Silu, t)
                b[q].done(tga)
        sa, sat = p.tile(a["ev_wa"], 1536)
        si, sit = p.tile(a["ev_wi"], 1536)
        for ch in range(12):
            o = xc[:, ch, :]
            z = lambda j: xa[:, ch, j:j + 256]
            cw = lambda j: p.c("ev_conv_w", j * 12 + ch)
            t = V.ts(o, z(0), cw(0), p.c("ev_conv_b", ch), MUL, ADD, tx, tz)
            for j in range(1, 4):
                t = V.stt(o, z(j), cw(j), o, MUL, ADD, t)
            bk = p.ps.get()
            P.mm(bk.t[:, 0:256], sa.t[:, ch * 128:(ch + 1) * 128], o, bk.free, t, sat)
            t2 = P.mm(bk.t[:, 256:512], si.t[:, ch * 128:(ch + 1) * 128], o, sit, start=False, sig=True)
            A.act(R[:, ch, :], bk.t[:, 0:256], ACT.Sigmoid, t2, bias=p.c("ev_b_a", ch))
            t3 = A.act(I[:, ch, :], bk.t[:, 256:512], ACT.Sigmoid, bias=p.c("ev_b_i", ch))
            bk.done(t3)
        sa.done(t2)
        si.done(t2)
        TH = xa
        tv = V.now()
        for ch in range(12):
            tt_ = A.act(TH[:, ch, 0:256], R[:, ch, :], ACT.Tanh, tv, A.now(), tc8, scale=c8[:, ch:ch + 1])
        ti = V.tt(I[:, :, :], I[:, :, :], xc[:, :, :], MUL, t3)
        for ch in range(12):
            ta = A.act(R[:, ch, :], R[:, ch, :], ACT.Exp, tt_, scale=c8[:, ch:ch + 1])
        for g in range(3):
            th = TH[:, 4 * g:4 * g + 4, 0:256]
            m4 = big[:, :].rearrange("p (c n) -> p c n", c=4)
            t1 = A.act(m4, th, ACT.Ln, tt_, V.now(), scale=-1.0, bias=1.0)
            t2 = V.ts(th, th, -2.0, 1e-18, MUL, MAX, t1)
            t3 = A.act(th, th, ACT.Ln, t2)
            t4 = V.tt(th, th, m4, SUB, t3)
            t5 = A.act(th, th, ACT.Exp, t4, scale=0.5)
            tu = V.tt(I[:, 4 * g:4 * g + 4, :], I[:, 4 * g:4 * g + 4, :], th, MUL, t5, ti)
        for ch in range(12):
            ts_ = V.do(lambda e, ch=ch: e.tensor_tensor_scan(xc[:, ch, :], R[:, ch, :], I[:, ch, :], 0.0, MUL, ADD),
                       ta, tu)
        ty = V.tt(xc[:, :, :], xc[:, :, :], ga[:, :, :], MUL, ts_, tga)
        b, t = p.proj(w, range(15 * 4, 16 * 4), "B")
        for q in range(2):
            tgb = A.act(gb[:, 2 * q:2 * q + 2, :], b[q].t.rearrange("p (c n) -> p c n", c=2), ACT.Silu, t)
            b[q].done(tgb)
        for nb in range(3):
            b, t = p.proj(w, range((12 + nb) * 4, (12 + nb) * 4 + 4), "A")
            for tt in range(2):
                tvv = A.act(vt[:, tt, nb * 512:(nb + 1) * 512], b[tt].t, ACT.Copy, t)
                b[tt].done(tvv)
        for which, dst in ((0, R), (1, I)):
            for nb in range(3):
                i0 = 6 + 3 * which + nb
                b, t = p.proj(w, range(i0 * 4, i0 * 4 + 4), "B")
                for q in range(2):
                    k = nb * 4 + q * 2
                    tq = A.act(dst[:, k:k + 2, :], b[q].t.rearrange("p (c n) -> p c n", c=2), ACT.Copy, t, ty,
                               scale=SQ if which == 0 else 1.0)
                    b[q].done(tq)
        tproj = t
        tdm = p.load("dm", dm[:, 0:M_N], a["dist"], tu, ty)
        to1 = p.to_lhs(xc[:, :, :], 0, 12, tproj, ty)
        SR = Ring([ga[:, 3 * i:3 * i + 3, :].rearrange("p c n -> p (c n)") for i in range(4)])
        PT = Ring([dm[:, M_N:M_N + 768], big[:, 0:768]])
        SR.slots[0].free = [ty]
        hold = {}

        def s1_(it):
            j, qt = it // 2, it % 2
            nk = 128 * (qt + 1)
            off = 128 * qt
            s = SR.get()
            b0, b1 = p.ps.get(), p.ps.get()
            P.wait(b0.free, b1.free, tq)
            for g in range(3):
                bk, o = (b0, g * 256) if g < 2 else (b1, 0)
                t = P.mm(bk.t[:, o:o + nk], R[:, g * 4 + j, off:off + 128], I[:, g * 4 + j, 0:nk],
                         start=(g != 1), sig=True)
            ts = []
            for g in range(3):
                bk, o = (b0, g * 256) if g < 2 else (b1, 0)
                mo = M_G[g] + (128 if qt else 0)
                ts.append(V.stt(s.t[:, g * nk:(g + 1) * nk], dm[:, mo:mo + nk], -SLOPE[g][j],
                                bk.t[:, o:o + nk], MUL, ADD, t, tdm, s.free, ty))
            b0.done(ts[1])
            b1.done(ts[2])
            mx, nm, den, rd = p.cell(), p.cell(), p.cell(), p.cell()
            t1 = V.red(mx, s.t[:, 0:3 * nk], MAX, ts)
            t2 = V.ts(nm, mx, -1.0, None, MUL, None, t1)
            t3 = A.act(s.t[:, 0:3 * nk], s.t[:, 0:3 * nk], ACT.Exp, t2, bias=nm, acc=den)
            hold[it] = (s, den, rd, t3)

        def s2_(it):
            j, qt = it // 2, it % 2
            nk = 128 * (qt + 1)
            s, den, rd, t3 = hold[it]
            t4 = V.rec(rd, den, t3)
            t5 = V.ts(s.t[:, 0:3 * nk], s.t[:, 0:3 * nk], rd, None, MUL, None, t4)
            pt = PT.get()
            n = 3 * nk // 128
            b0 = p.ps.get()
            b1 = p.ps.get() if n > 4 else None
            P.wait(b0.free, t5, b1.free if b1 else None)
            for i in range(n):
                bk = b0 if i < 4 else b1
                t = P.tr(bk.t[:, (i % 4) * 128:(i % 4) * 128 + 128], s.t[:, i * 128:(i + 1) * 128], p.ident, sig=True)
            s.done(t)
            m = min(n, 4)
            t6 = A.act(pt.t[:, 0:m * 128], b0.t[:, 0:m * 128], ACT.Copy, t, pt.free)
            b0.done(t6)
            if b1:
                t6 = A.act(pt.t[:, 512:n * 128], b1.t[:, 0:(n - 4) * 128], ACT.Copy)
                b1.done(t6)
            hold[it] = (pt, t6)

        def s3_(it):
            j, qt = it // 2, it % 2
            kt = qt + 1
            pt, t6 = hold[it]
            bk = p.ps.get()
            P.wait(bk.free, t6, tvv)
            for g in range(3):
                for x in range(kt):
                    i = g * kt + x
                    hd = g * 4 + j
                    t = P.mm(bk.t[:, 0:128], vt[:, x, hd * 128:(hd + 1) * 128], pt.t[:, i * 128:(i + 1) * 128],
                             start=(i == 0), stop=(i == 3 * kt - 1), sig=True)
            pt.done(t)
            y = gb[:, j, qt * 128:(qt + 1) * 128]
            ty2 = V.tt(y, bk.t[:, 0:128], y, MUL, t, tgb)
            bk.done(ty2)
            hold["y"] = ty2

        skew(8, [s1_, s2_, s3_])
        to2 = p.to_lhs(gb[:, :, :], 12, 4, hold["y"], tproj)
        p.x_t = [p.out_residual(a["ev_out"], [to1, to2])]


def layer2(p, a):
    V, A, P, G = p.V, p.A, p.P, p.G
    with ExitStack() as c:
        sb = lambda n, s: p.sb("l2" + n, s, F32, c)
        q = sb("q", [128, 1024])
        k = sb("k", [128, 1024])
        b_ = sb("b", [128, 1024])
        vt = sb("v", [128, 2, 1024])
        gc = sb("gc", [128, 2, 1024])
        u = sb("u", [128, 2, 1024])
        vd = sb("vd", [128, 2, 1024])
        gd = sb("gd", [128, 2, 1024])
        p.junk = sb("junk", [128, 1024])
        E1 = sb("e1", [128, 1024])
        E2 = sb("e2", [128, 1024])
        At = sb("at", [128, 1024])
        Ac = sb("ac", [128, 512])
        hn = sb("hn", [128, 1024])
        vn = sb("vn", [128, 1024])
        bt = p.barrier()
        th = p.load("hn", hn[:, :], a["head_norm"], bt)
        tvn = p.load("vn", vn[:, :], a["v_norm"], bt)
        tws = p.load("ws", Ac[:, :], a["w_s"], bt)
        twal = p.load("wal", E2[0:16, 0:512], a["w_alpha"], bt)

        class XN:
            def __getitem__(self, kk):
                z = u if kk[1] == 0 else vd
                return z[:, :, :].rearrange("p a n -> p (a n)")[:, kk[2]]

        lt = p.norm_T(XN(), "od_norm", p.x_t)
        w = a["od_in"]
        ti = [0]

        def blk(mode):
            r = p.proj(w, range(ti[0], ti[0] + 4), mode, lt=lt)
            ti[0] += 4
            return r

        for dst, sc in ((q, SQ), (k, 1.0)):
            b, t = blk("B")
            for i in range(2):
                tq = A.act(dst[:, i * 512:(i + 1) * 512], b[i].t, ACT.Copy, t, scale=sc)
                b[i].done(tq)

        def tok(dst, func):
            for nb in range(2):
                b, t = blk("A")
                for tt in range(2):
                    te = A.act(dst[:, tt, nb * 512:(nb + 1) * 512], b[tt].t, func, t, V.now())
                    b[tt].done(te)
            return te

        bs, t = p.proj_small(a["od_alr"], 16, lt)
        al = E1[:, 0:32]
        t1 = A.act(al.rearrange("p (a n) -> p a n", a=2), bs.t[:, 0:128].rearrange("p (a n) -> p a n", a=2)[:, :, 0:16],
                   ACT.Copy, t)
        bs.done(t1)
        bk = p.ps.get()
        P.wait(bk.free, t1)
        for tt in range(2):
            t = P.mm(bk.t[0:16, tt * 128:(tt + 1) * 128], al[:, tt * 16:(tt + 1) * 16], p.ident, start=(tt == 0), sig=True)
        alT = E1[0:16, 256:512]
        t2 = A.act(alT, bk.t[0:16, 0:256], ACT.Copy, t)
        bk.done(t2)
        bks = [p.ps.get(), p.ps.get()]
        P.wait(t2, twal, bks[0].free, bks[1].free)
        for h in range(4):
            t = P.mm(bks[h // 2].t[:, (h % 2) * 256:(h % 2) * 256 + 256], E2[0:16, h * 128:(h + 1) * 128], alT,
                     start=(h % 2 == 0), sig=True)
        for h in range(4):
            t3 = V.ts(b_[:, h * 256:(h + 1) * 256], bks[h // 2].t[:, (h % 2) * 256:(h % 2) * 256 + 256],
                      p.c("od_b_alpha", h), None, ADD, None, t)
        bks[0].done(t3)
        bks[1].done(t3)
        ab = At[:, :]
        t4 = V.stt(ab, b_[:, :], -1.0, b_[:, :], MUL, MAX, t3)
        t5 = A.act(ab, ab, ACT.Exp, t4, scale=-1.0)
        t6 = A.act(ab, ab, ACT.Ln, t5, bias=1.0)
        t7 = V.stt(b_[:, :], b_[:, :], 0.0, ab, MIN, SUB, t6)
        t8 = V.ts(At[:, :], b_[:, :], 1.0 / 16.0, None, MUL, None, t7)
        for h in range(4):
            t9 = V.do(lambda e, h=h: e.tensor_tensor_scan(b_[:, h * 256:(h + 1) * 256], At[:, h * 256:(h + 1) * 256],
                                                          At[:, h * 256:(h + 1) * 256], 0.0, ADD, ALU.bypass), t8)
        tv = tok(vt, ACT.Copy)
        tg = tok(gc, ACT.Silu)
        tu = tok(u, ACT.Gelu_apprx_tanh)
        tvd = tok(vd, ACT.Gelu_apprx_tanh)
        tgd = tok(gd, ACT.Silu)
        tl = None
        for tt in range(2):
            z = vd[:, tt, :].rearrange("p (g e) -> p g e", g=4)
            mu, ss = p.cell(4), p.cell(4)
            t1 = V.red(mu, z, ADD, tvd)
            t1 = V.ts(mu, mu, 1.0 / 256, None, MUL, None, t1)
            t2 = V.tt(z, z, bc(mu.unsqueeze(2), [128, 4, 256]), SUB, t1)
            t3 = A.act(p.junk[:, :], vd[:, tt, :], ACT.Square, t2, V.now())
            t4 = V.red(ss, p.junk[:, :].rearrange("p (g e) -> p g e", g=4), ADD, t3)
            r, t5 = p.rsqrt(ss, 4, 1.0 / 256, t4)
            t6 = V.tt(z, z, bc(r.unsqueeze(2), [128, 4, 256]), MUL, t5)
            t7 = V.tt(vd[:, tt, :], vd[:, tt, :], vn[:, :], MUL, t6, tvn)
            ug = V.tt(u[:, tt, :], u[:, tt, :], gd[:, tt, :], MUL, tu, tgd)
            if tt == 0:
                wsm = V.tt(Ac[:, :].rearrange("p (g t) -> p g t", g=4), Ac[:, :].rearrange("p (g t) -> p g t", g=4),
                           bc(p.cst[:, C_TRI:C_TRI + 128].unsqueeze(1), [128, 4, 128]), MUL, tws)
            for g in range(0, 4, 2):
                bk = p.ps.get()
                P.wait(bk.free, t7, wsm)
                for i in range(2):
                    t = P.mm(bk.t[:, i * 256:(i + 1) * 256], Ac[:, (g + i) * 128:(g + i + 1) * 128],
                             vd[:, tt, (g + i) * 256:(g + i + 1) * 256], start=(i == 0), sig=True)
                for i in range(2):
                    us = u[:, tt, (g + i) * 256:(g + i + 1) * 256]
                    tl = V.stt(us, bk.t[:, i * 256:(i + 1) * 256], p.c("od_b_s", g + i), us, ADD, MUL, t, ug)
                bk.done(tl)
        tproj = P.now()
        t_yd = p.turn(u, 8, 8, tl, tproj)
        tT = P.now()
        o = gd
        to = p.decay_attention(q[:, :], k[:, :], b_[:, :], vt, o, 4, 256, [E1[:, :], E2[:, :]], At, Ac,
                               [t9, tq, t8, tv, tT, tl], [tl])
        to = p.headnorm(o, 4, 256, hn[:, :], gc, to, th, tg)
        t_yc = p.turn(o, 0, 8, to)
        p.x_t = [p.out_residual(a["od_out"], [t_yd, t_yc])]


def final_first(p, a):
    V = p.V
    with ExitStack() as c:
        g = p.sb("fng", [128, D], F32, c)
        p.junk = p.sb("fnj", [128, D], F32, c)
        bt = p.barrier()
        tg = p.load("fn", g[:, :], a["final_norm"], bt)
        for tt in range(2):
            xs = p.x[:, tt, :]
            r, t = p.row_rstd(xs, p.junk[:, :], tt, p.x_t if tt == 0 else None)
            t = V.stt(xs, xs, r, g[:, :], MUL, MUL, t, tg)
        p.x_t = [t]


def layer3(p, a):
    V, A, P, G = p.V, p.A, p.P, p.G
    with ExitStack() as c:
        sb = lambda n, s, cc=c: p.sb("l3" + n, s, F32, cc)
        oa = sb("oa", [128, 2, 1024])
        gn = sb("gn", [128, 256])
        p.junk = sb("junk", [128, 1024])
        w = a["ab_in"]
        with ExitStack() as c2:
            q = sb("q", [128, 2048], c2)
            k = sb("k", [128, 2048], c2)
            b_ = sb("b", [128, 2048], c2)
            vt = sb("v", [128, 2, 1024], c2)
            ag = sb("ag", [128, 2, 1024], c2)
            E1 = sb("e1", [128, 2048], c2)
            E2 = sb("e2", [128, 2048], c2)
            At = sb("at", [128, 2048], c2)
            Ac = sb("ac", [128, 1024], c2)
            bt = p.barrier()
            tgn = p.load("gn", gn[:, :], a["gn3"], bt)

            class XN:
                def __getitem__(self, kk):
                    return (E1 if kk[1] == 0 else E2)[:, kk[2]]

            lt = p.norm_T(XN(), "norm00", p.x_t)
            lgt = p.c("lb", 0, 8)
            e1, e2, lb, oml = p.cell(8), p.cell(8), p.cell(8), p.cell(8)
            t = V.tt(e1, lgt, lgt, SUB, p.cst_t)
            t = A.act(e1, e1, ACT.Exp, t)
            t = V.rec(e2, e1, t)
            t = V.tt(e1, e1, e2, MUL, t)
            t = V.tt(lb, e1, e1, SUB, t)
            tlb = V.ts(oml, lb, -1.0, 1.0, MUL, ADD, t)

            def blkB(i, dst, func, *ww):
                b, t = p.proj(w, range(i * 4, i * 4 + 4), "B", lt=lt)
                for h in range(2):
                    te = A.act(dst[:, h * 512:(h + 1) * 512], b[h].t, func, t, *ww)
                    b[h].done(te)
                return te

            def blkA(i, dst, func, off, *ww):
                b, t = p.proj(w, range(i * 4, i * 4 + 4), "A", lt=lt)
                for tt in range(2):
                    te = A.act(dst[:, tt, off:off + 512], b[tt].t, func, t, *ww)
                    b[tt].done(te)
                return te

            for i in range(2):
                tf = blkB(2 + i, b_[:, i * 1024:(i + 1) * 1024], ACT.Sigmoid)
            for i in range(2):
                tq = blkB(i, q[:, i * 1024:(i + 1) * 1024], ACT.Copy)
            for h in range(8):
                s = slice(h * 256, (h + 1) * 256)
                t1 = V.ts(b_[:, s], b_[:, s], oml[:, h:h + 1], lb[:, h:h + 1], MUL, ADD, tf, tlb)
            t2 = V.ts(k[:, :], b_[:, :], -1.0, 1.0, MUL, ADD, t1)
            t3 = V.ts(At[:, :], b_[:, :], 2.0 ** -63, None, MAX, None, t1)
            t4 = A.act(At[:, :], At[:, :], ACT.Ln, t3)
            for h in range(8):
                s = slice(h * 256, (h + 1) * 256)
                t9 = V.do(lambda e, s=s: e.tensor_tensor_scan(b_[:, s], At[:, s], At[:, s], 0.0, ADD, ALU.bypass), t4, t2)
            for i in range(2):
                tv = blkA(4 + i, vt, ACT.Copy, i * 512)
            for i in range(2):
                tg = blkA(6 + i, ag, ACT.Silu, i * 512)
            to = p.decay_attention(q[:, :], k[:, :], b_[:, :], vt, oa, 8, 128, [E1[:, :], E2[:, :]], At, Ac,
                                   [t9, tq, tv, t4])
            toa = p.headnorm(oa, 8, 128, gn[:, 0:128], ag, to, tgn, tg)
        with ExitStack() as c2:
            z = sb("z", [128, 8, 260], c2)
            qk = sb("qk", [128, 16, 256], c2)
            vb = sb("vb", [128, 2, 1024], c2)
            bg = sb("bg", [128, 2, 1024], c2)
            ob = vb
            sm = sb("sm", [128, 2, 48], c2)
            kb = sb("kb", [128, 1024], c2)
            W = sb("w", [128, 4096], c2)
            bt = p.barrier()
            tz = V.do(lambda e: e.memset(z[:, :, 0:3], 0.0))
            vT = W[:, 0:2048].rearrange("p (c n) -> p c n", c=8)
            tk, tc = None, None
            for part in range(3):
                dst = qk[:, part * 8:part * 8 + 8, :] if part < 2 else vT
                for nb in range(2):
                    i = 8 + part * 2 + nb
                    b, t = p.proj(w, range(i * 4, i * 4 + 4), "B", lt=lt)
                    for q_ in range(2):
                        kk = nb * 4 + q_ * 2
                        tk = A.act(z[:, kk:kk + 2, 3:259], b[q_].t.rearrange("p (c n) -> p c n", c=2), ACT.Copy, t, tc)
                        b[q_].done(tk)
                for ch in range(8):
                    o = dst[:, ch, :]
                    t = None
                    for j in range(4):
                        cw = p.c("gdn_conv", j * 24 + part * 8 + ch)
                        zz = z[:, ch, j:j + 256]
                        if j == 0:
                            t = V.ts(o, zz, cw, None, MUL, None, tk, tz)
                        else:
                            t = V.stt(o, zz, cw, o, MUL, ADD, t)
                tc = t
                tsl = A.act(dst, dst, ACT.Silu, tc)
                if part == 1:
                    tqk = tsl
            for i in range(2):
                b, t = p.proj(w, range((14 + i) * 4, (14 + i) * 4 + 4), "A", lt=lt)
                for tt in range(2):
                    tg = A.act(bg[:, tt, i * 512:(i + 1) * 512], b[tt].t, ACT.Silu, t)
                    b[tt].done(tg)
            bs, t = p.proj_small(a["ab_small"], 16, lt)
            bv = bs.t[:, 0:128].rearrange("p (a n) -> p a n", a=2)
            ea = p.cell(8)
            te = A.act(ea, p.c("a_log", 0, 8), ACT.Exp)
            t1 = V.tt(sm[:, :, 0:8], bv[:, :, 0:8], bc(p.c("dt_bias", 0, 8).unsqueeze(1), [128, 2, 8]), ADD, t)
            t2 = A.act(sm[:, :, 8:16], bv[:, :, 8:16], ACT.Sigmoid, t, t1)
            bs.done(t1, t2)
            t3 = V.stt(sm[:, :, 16:24], sm[:, :, 0:8], -1.0, sm[:, :, 0:8], MUL, MAX, t1)
            t4 = A.act(sm[:, :, 16:24], sm[:, :, 16:24], ACT.Exp, t3, scale=-1.0)
            t5 = A.act(sm[:, :, 16:24], sm[:, :, 16:24], ACT.Ln, t4, bias=1.0)
            t6 = V.stt(sm[:, :, 0:8], sm[:, :, 0:8], 0.0, sm[:, :, 16:24], MAX, ADD, t5)
            t7 = V.tt(sm[:, :, 0:8], sm[:, :, 0:8], bc(ea.unsqueeze(1), [128, 2, 8]), MUL, t6, te)
            tld = V.ts(sm[:, :, 0:8], sm[:, :, 0:8], -1.0, None, MUL, None, t7)
            beta = lambda tt, h: sm[:, tt, 8 + h:9 + h]
            tri = p.cst[:, C_TRI:C_TRI + 128]
            one = p.cst[:, C_ONE:C_ONE + 128]
            bk = p.ps.get()
            P.mm(bk.t[:, 0:8], tri, sm[:, 0, 0:8], bk.free, tld)
            P.mm(bk.t[:, 8:16], one, sm[:, 0, 0:8], start=False)
            t = P.mm(bk.t[:, 8:16], tri, sm[:, 1, 0:8], start=False, sig=True)
            tgc = A.act(sm[:, :, 24:32], bk.t[:, 0:16].rearrange("p (a n) -> p a n", a=2), ACT.Copy, t)
            bk.done(tgc)
            gcol = lambda tt, h: sm[:, tt, 24 + h:25 + h]
            for hh in range(0, 8, 2):
                bk = p.ps.get()
                P.wait(bk.free, tsl)
                for i in range(2):
                    for tt in range(2):
                        t = P.tr(bk.t[:, (i * 2 + tt) * 128:(i * 2 + tt + 1) * 128],
                                 vT[:, hh + i, tt * 128:(tt + 1) * 128], p.ident, sig=True)
                for i in range(2):
                    for tt in range(2):
                        tvb = V.ts(vb[:, tt, (hh + i) * 128:(hh + i + 1) * 128],
                                   bk.t[:, (i * 2 + tt) * 128:(i * 2 + tt + 1) * 128], beta(tt, hh + i), None,
                                   MUL, None, t, t2)
                bk.done(tvb)
            tn = [tvb]
            for g in range(0, 16, 2):
                s = W[:, 2048 + (g // 2 % 2) * 512:2560 + (g // 2 % 2) * 512]
                x2 = qk[:, g:g + 2, :].rearrange("p c n -> p (c n)")
                t1 = A.act(s, x2, ACT.Square, tqk, tn[-2] if len(tn) > 1 else None)
                bk = p.ps.get()
                t2_ = P.mm(bk.t, one, s, t1, bk.free, sig=True)
                t3 = A.act(s, bk.t, ACT.Ln, t2_, bias=p.cst[:, C_EPS:C_EPS + 1])
                bk.done(t3)
                t4 = A.act(s, s, ACT.Exp, t3, scale=-0.5)
                tn.append(V.stt(x2, x2, SQ if g < 8 else 1.0, s, MUL, MUL, t4))
            tn = [tn[-1]]
            iv = lambda ap, n: ap.rearrange("p (i t) -> p i t", i=n)
            DT = W[:, 0:1536]
            LT = W[:, 1536:3072]
            Tm = W[:, 3072:4096]
            AT = z[:, :, :].rearrange("p c n -> p (c n)")[:, 0:1536]
            hv = p.junk
            lev = lambda l: p.cst[:, C_LEV + l * 128:C_LEV + (l + 1) * 128]
            with ExitStack() as c3:
                Tt = sb("tt", [128, 1024], c3)
                Mx = sb("mx", [128, 1024], c3)
                prev = [V.now(), A.now(), P.now()]
                for half in range(2):
                    H0 = half * 4
                    for h in range(4):
                        lb_ = Mx[:, (h % 2) * 512:(h % 2) * 512 + 256]
                        bb_ = Mx[:, (h % 2) * 512 + 256:(h % 2) * 512 + 512]
                        t0 = V.cp(lb_.rearrange("p (a n) -> p a n", a=2),
                                  bc(sm[:, :, H0 + h:H0 + h + 1], [128, 2, 128]), tld, prev, P.now())
                        t1 = V.cp(bb_.rearrange("p (a n) -> p a n", a=2),
                                  bc(sm[:, :, 8 + H0 + h:9 + H0 + h], [128, 2, 128]), prev)
                        bk = p.ps.get()
                        P.mm(bk.t[:, 0:256], lb_[:, 0:128], p.cst[:, C_TRI:C_TRI + 256], bk.free, t0, t1)
                        P.mm(bk.t[:, 0:256], lb_[:, 128:256], p.cst[:, C_ZERO:C_ZERO + 256], start=False)
                        for tt in range(2):
                            t = P.mm(bk.t[:, 256 + tt * 128:384 + tt * 128], bb_[:, tt * 128:(tt + 1) * 128], p.ident,
                                     start=False, sig=True)
                        d = h * 384
                        V.ts(DT[:, d:d + 256], bk.t[:, 0:256], gcol(0, H0 + h), 0.0, SUB, MIN, t, tgc, prev)
                        V.ts(DT[:, d + 256:d + 384], bk.t[:, 128:256], gcol(1, H0 + h), 0.0, SUB, MIN)
                        tkb = V.tt(kb[:, h * 256:(h + 1) * 256], qk[:, 8 + H0 + h, :], bk.t[:, 256:512], MUL, tn)
                        bk.done(tkb)
                    te = A.act(DT, DT, ACT.Exp, V.now())
                    d4 = DT.rearrange("p (h b t) -> p h b t", h=4, b=3)
                    td = None
                    for bi in (0, 2):
                        td = V.tt(d4[:, :, bi, :], d4[:, :, bi, :], bc(tri.unsqueeze(1), [128, 4, 128]), MUL, te)
                    for h in range(4):
                        kT = qk[:, 8 + H0 + h, :]
                        qT = qk[:, H0 + h, :]
                        kbT = kb[:, h * 256:(h + 1) * 256]
                        d = h * 384
                        for dst, rhs in ((LT, kbT), (AT, qT)):
                            bk = p.ps.get()
                            P.mm(bk.t[:, 0:256], kT[:, 0:128], rhs, bk.free, tkb, tn)
                            t = P.mm(bk.t[:, 256:384], kT[:, 128:256], rhs[:, 128:256], start=False, sig=True)
                            tl = V.tt(dst[:, d:d + 384], bk.t[:, 0:384], DT[:, d:d + 384], MUL, t, td, prev)
                            bk.done(tl)
                    L4 = LT.rearrange("p (h b t) -> p h b t", h=4, b=3)
                    diag = lambda tt: L4[:, :, tt * 2, :]
                    v4 = lambda ap, tt: ap.rearrange("p (h a t) -> p h a t", h=4, a=2)[:, :, tt, :]
                    m4 = lambda l: bc(lev(l).unsqueeze(1), [128, 4, 128])
                    for tt in range(2):
                        t1 = V.tt(v4(Tt[:, :], tt), diag(tt), m4(0), MUL, tl, prev)
                        t1 = V.tt(v4(Tt[:, :], tt), bc(p.ident.unsqueeze(1), [128, 4, 128]), v4(Tt[:, :], tt), SUB, t1)
                    for g in range(2):
                        bk = p.ps.get()
                        P.wait(bk.free, t1)
                        for i in range(4):
                            t = P.tr(bk.t[:, i * 128:(i + 1) * 128], inst_at(Tt, g * 4 + i), p.ident, sig=True)
                        tT = A.act(Tm[:, g * 512:(g + 1) * 512], bk.t, ACT.Copy, t, prev)
                        bk.done(tT)
                    ttt = t1
                    LM = DT[:, 0:1024]
                    for level in range(1, 7):
                        for tt in range(2):
                            tm = G.tt(v4(LM, tt), diag(tt), m4(level), MUL, tl, P.now())
                        tM, banks = [], []
                        for g in range(2):
                            bk = p.ps.get()
                            P.wait(bk.free, tm, tT)
                            for i in range(4):
                                t = P.mm(bk.t[:, i * 128:(i + 1) * 128], inst_at(LM, g * 4 + i), inst_at(Tm, g * 4 + i),
                                         start=(i == 0), sig=True)
                            tm_ = A.act(Mx[:, g * 512:(g + 1) * 512], bk.t, ACT.Copy, t)
                            bk.done(tm_)
                            tM.append(tm_)
                        nt, nT = [], []
                        for g in range(2):
                            b1 = p.ps.get()
                            b2 = p.ps.get() if level < 6 else None
                            P.wait(b1.free, b2.free if b2 else None, tM[g], ttt)
                            for i in range(4):
                                j = g * 4 + i
                                t = P.mm(b1.t[:, i * 128:(i + 1) * 128], inst_at(Mx, j), inst_at(Tt, j),
                                         start=(i == 0), sig=True)
                            if b2:
                                for i in range(4):
                                    j = g * 4 + i
                                    t = P.mm(b2.t[:, i * 128:(i + 1) * 128], inst_at(Tt, j), inst_at(Mx, j),
                                             start=(i == 0), sig=True)
                            s = slice(g * 512, (g + 1) * 512)
                            ttt = V.tt(Tt[:, s], Tt[:, s], b1.t, SUB, t)
                            b1.done(ttt)
                            if b2:
                                tT = V.tt(Tm[:, s], Tm[:, s], b2.t, SUB, t)
                                b2.done(tT)
                    tfin = ttt
                    U = Mx[:, :]
                    hs = slice(H0 * 128, H0 * 128 + 512)
                    bk = p.ps.get()
                    P.wait(bk.free, tfin)
                    for h in range(4):
                        t = P.mm(bk.t[:, h * 128:(h + 1) * 128], inst_at(Tt, h * 2),
                                 vb[:, 0, (H0 + h) * 128:(H0 + h + 1) * 128], start=(h == 0), sig=True)
                    t1 = A.act(U[:, 0:512], bk.t, ACT.Copy, t)
                    bk.done(t1)
                    bk = p.ps.get()
                    P.wait(bk.free, t1)
                    for h in range(4):
                        t = P.mm(bk.t[:, h * 128:(h + 1) * 128], LT[:, h * 384 + 128:h * 384 + 256],
                                 U[:, h * 128:(h + 1) * 128], start=(h == 0), sig=True)
                    t2_ = V.tt(vb[:, 1, hs], vb[:, 1, hs], bk.t, SUB, t)
                    bk.done(t2_)
                    bk = p.ps.get()
                    P.wait(bk.free, t2_)
                    for h in range(4):
                        t = P.mm(bk.t[:, h * 128:(h + 1) * 128], inst_at(Tt, h * 2 + 1),
                                 vb[:, 1, (H0 + h) * 128:(H0 + h + 1) * 128], start=(h == 0), sig=True)
                    t3 = A.act(U[:, 512:1024], bk.t, ACT.Copy, t)
                    bk.done(t3)
                    for tt in range(2):
                        bk = p.ps.get()
                        P.wait(bk.free, t1, t3)
                        for h in range(4):
                            out = bk.t[:, h * 128:(h + 1) * 128]
                            d = h * 384
                            if tt == 0:
                                t = P.mm(out, AT[:, d:d + 128], U[:, h * 128:(h + 1) * 128], start=(h == 0), sig=True)
                            else:
                                P.mm(out, AT[:, d + 128:d + 256], U[:, h * 128:(h + 1) * 128], start=(h == 0), stop=False)
                                t = P.mm(out, AT[:, d + 256:d + 384], U[:, 512 + h * 128:512 + (h + 1) * 128],
                                         start=False, sig=True)
                        to = A.act(ob[:, tt, hs], bk.t, ACT.Copy, t)
                        bk.done(to)
                    prev = [V.now(), A.now(), P.now()]
            tob = p.headnorm(ob, 8, 128, gn[:, 128:256], bg, to, tg)
            t1 = p.turn(oa, 0, 8, toa, P.now())
            t2 = p.turn(ob, 8, 8, tob)
        with ExitStack() as c2:
            m = p.sb("l3m", [128, 2, D], F32, c2)
            gbc = p.sb("l3g", [128, D], F32, c2)
            p.junk = p.sb("l3j", [128, D], F32, c2)
            bt = p.barrier()
            gt = p.load("gbc", gbc[:, :], a["g_post01"], bt)
            p.x_t = p.out_post(a["ab_out"], [t1, t2], m, gbc[:, :], gt)


def layer4(p, a):
    V, A, P, G = p.V, p.A, p.P, p.G
    with ExitStack() as c:
        sb = lambda n, s, cc=c: p.sb("l4" + n, s, F32, cc)
        qT = sb("q", [128, 16, 256])
        ks = sb("ks", [128, 4, 256])
        kw = sb("kw", [128, 4, 256])
        kc = sb("kc", [128, 4, 256])
        vc = sb("vc", [128, 4, 256])
        vs = sb("vs", [128, 2, 512])
        vw = sb("vw", [128, 2, 512])
        gl = sb("gl", [128, 2, 48])
        dm = sb("dm", [128, 384 + 64])
        rhs = sb("rh", [128, 1920])
        hT = sb("ht", [128, 128])
        kcm = sb("kcm", [128, 64])
        vcm = sb("vcm", [16, 512])
        w2 = sb("w2", [128, 256])
        SR = Ring([sb(f"s{i}", [128, 528])[:, :] for i in range(4)])
        PT = Ring([sb(f"pt{i}", [128, 640])[:, :] for i in range(3)])
        bt = p.barrier()
        tdm = p.load("dm4", dm[:, :], a["dist4"], bt)
        tw2 = p.load("w2", w2[:, :], a["cmp_w2"], bt)

        class XN:
            def __getitem__(self, kk):
                return qT[:, :, :].rearrange("p c n -> p (c n)")[:, kk[1] * 2048:(kk[1] + 1) * 2048][:, kk[2]]

        lt = p.norm_T(XN(), "norm10", p.x_t)
        w = a["nsa_in"]
        order = [(4, kc, 1.0), (5, vc, 1.0), (6, ks, 1.0), (8, kw, 1.0)]
        for i, dst, sc in order:
            b, t = p.proj(w, range(i * 4, i * 4 + 4), "B", lt=lt)
            for h in range(2):
                tk = A.act(dst[:, 2 * h:2 * h + 2, :], b[h].t.rearrange("p (c n) -> p c n", c=2), ACT.Copy, t)
                b[h].done(tk)
        for i, dst in ((7, vs), (9, vw)):
            b, t = p.proj(w, range(i * 4, i * 4 + 4), "A", lt=lt)
            for tt in range(2):
                tv = A.act(dst[:, tt, :], b[tt].t, ACT.Copy, t)
                b[tt].done(tv)
        for which, src in ((0, kc), (1, vc)):
            r4 = rhs[:, :].rearrange("p (g j l) -> p g j l", g=4, j=15)
            hv = hT[:, which * 64:which * 64 + 60]
            t = P.now()
            pos = p.c(f"pos{which}", 0, 32)
            for g in range(4):
                s3 = src[:, g, :].rearrange("p (j l) -> p j l", l=16)
                for half in range(2):
                    tr = V.tt(r4[:, g, :, half * 16:half * 16 + 16], s3[:, half:half + 15, :],
                              bc(pos[:, half * 16:half * 16 + 16].unsqueeze(1), [128, 15, 16]), ADD, tk, t)
            rl = rhs[:, :].rearrange("p (n l) -> p l n", l=32)
            bk = p.ps.get()
            P.wait(bk.free, tr)
            for half in range(2):
                s, st = p.tile(a["cmp_w1"][which * 2 + half])
                P.wait(st)
                for l in range(16):
                    ll = half * 16 + l
                    t = P.mm(bk.t[:, 0:60], s.t[:, l * 128:(l + 1) * 128], rl[:, ll, :], start=(ll == 0),
                             stop=(ll == 31), sig=(l == 15))
                s.done(t)
            th = A.act(hv, bk.t[:, 0:60], ACT.Silu, t)
            bk.done(th)
            bk = p.ps.get()
            P.wait(bk.free, th, tw2)
            if which == 0:
                t = P.mm(bk.t[:, 0:60], w2[:, 0:128], hv, sig=True)
                tkc = A.act(kcm[:, 0:60], bk.t[:, 0:60], ACT.Copy, t)
                bk.done(tkc)
            else:
                for g in range(4):
                    t = P.mm(bk.t[0:15, g * 128:(g + 1) * 128], hv[:, g * 15:(g + 1) * 15], w2[:, 128:256],
                             start=(g == 0), sig=True)
                tvc = A.act(vcm[0:15, :], bk.t[0:15, :], ACT.Copy, t)
                bk.done(tvc)
        bs, t = p.proj_small(a["nsa_small"], 48, lt)
        tgl = A.act(gl[:, :, :], bs.t[:, 0:128].rearrange("p (a n) -> p a n", a=2)[:, :, 0:48], ACT.Sigmoid, t)
        bs.done(tgl)
        for i in range(4):
            b, t = p.proj(w, range(i * 4, i * 4 + 4), "B", lt=lt)
            for h in range(2):
                k = i * 4 + 2 * h
                tq = A.act(qT[:, k:k + 2, :], b[h].t.rearrange("p (c n) -> p c n", c=2), ACT.Copy, t, scale=SQ)
                b[h].done(tq)
        tproj = t
        hold = {}

        def s1_(it):
            h, qt = it // 2, it % 2
            g = h // 4
            nk = 128 * (qt + 1)
            q = qT[:, h, qt * 128:(qt + 1) * 128]
            s = SR.get()
            b0, b1 = p.ps.get(), p.ps.get()
            P.wait(b0.free, b1.free, tq, tk, tkc)
            P.mm(b0.t[:, 0:nk], q, ks[:, g, 0:nk])
            P.mm(b0.t[:, 256:256 + nk], q, kw[:, g, 0:nk], start=False)
            t = P.mm(b1.t[:, 0:15], q, kcm[:, g * 15:(g + 1) * 15], sig=True)
            mo = 128 if qt else 0
            d3 = bc(dm[:, mo:mo + nk].unsqueeze(1), [128, 2, nk])
            s3 = s.t[:, 0:2 * nk].rearrange("p (a n) -> p a n", a=2)
            p3 = b0.t.rearrange("p (a n) -> p a n", a=2)[:, :, 0:nk]
            t1 = V.stt(s3, d3, -SLOPE2[h], p3, MUL, ADD, t, tdm, s.free)
            b0.done(t1)
            sc = s.t[:, 512:527]
            t2 = V.stt(sc, dm[:, 384 + qt * 16:384 + qt * 16 + 15], -SLOPE2[h], b1.t[:, 0:15], MUL, ADD, t, s.free)
            b1.done(t2)
            mx, den, rg = p.cell(3), p.cell(3), p.cell(3)
            t3 = V.do(lambda e: e.tensor_reduce(mx[:, 0:2], s3, AX.X, MAX), t1)
            t4 = V.red(mx[:, 2:3], sc, MAX, t2)
            t5 = V.ts(mx, mx, -1.0, None, MUL, None, t3, t4)
            ap = [s.t[:, 0:nk], s.t[:, nk:2 * nk], sc]
            for i in range(3):
                t6 = A.act(ap[i], ap[i], ACT.Exp, t5, bias=mx[:, i:i + 1], acc=den[:, i:i + 1])
            hold[it] = (s, den, rg, t6, ap)

        def s2_(it):
            h, qt = it // 2, it % 2
            nk = 128 * (qt + 1)
            s, den, rg, t6, ap = hold[it]
            t1 = V.rec(rg, den, t6)
            g3 = gl[:, qt, 3 * h:3 * h + 3]
            gw = [g3[:, 1:2], g3[:, 2:3], g3[:, 0:1]]
            for i in range(2):
                t2 = V.ts(ap[i], ap[i], rg[:, i:i + 1], gw[i], MUL, MUL, t1, tgl)
            t2 = V.ts(ap[2], ap[2], rg[:, 2:3], gw[2], MUL, MUL, t1, tgl)
            v0 = 384 + 32 + qt * 16
            t3 = V.tt(ap[2], ap[2], dm[:, v0:v0 + 15], MUL, t2)
            n = 2 * nk // 128
            b0, b1 = p.ps.get(), p.ps.get()
            P.wait(b0.free, b1.free, t3)
            for i in range(n):
                t = P.tr(b0.t[:, i * 128:(i + 1) * 128], s.t[:, i * 128:(i + 1) * 128], p.ident)
            t = P.tr(b1.t[0:15, 0:128], ap[2], p.ident, sig=True)
            s.done(t)
            pt = PT.get()
            t4 = A.act(pt.t[:, 0:n * 128], b0.t[:, 0:n * 128], ACT.Copy, t, pt.free)
            b0.done(t4)
            t5 = A.act(pt.t[0:15, 512:640], b1.t[0:15, 0:128], ACT.Copy, t)
            b1.done(t5)
            hold[it] = (pt, t5, n)

        def s3_(it):
            h, qt = it // 2, it % 2
            g = h // 4
            pt, t5, n = hold[it]
            bk = p.ps.get()
            P.wait(bk.free, t5, tv, tvc)
            gs = slice(g * 128, (g + 1) * 128)
            kt = qt + 1
            for i in range(n):
                src = vs if i < kt else vw
                P.mm(bk.t[:, 0:128], src[:, i % kt, gs], pt.t[:, i * 128:(i + 1) * 128], start=(i == 0), stop=False)
            t = P.mm(bk.t[:, 0:128], vcm[0:15, gs], pt.t[0:15, 512:640], start=False, sig=True)
            pt.done(t)
            o = slice(qt * 128, (qt + 1) * 128)
            th = A.act(p.xhi[:, h, o], bk.t[:, 0:128], ACT.Copy, t, tproj)
            tl = V.tt(p.xlo[:, h, o], bk.t[:, 0:128], p.xhi[:, h, o].bitcast(F32), SUB, th)
            bk.done(tl)
            hold["o"] = [th, tl]

        skew(32, [s1_, s2_, s3_])
        lt2 = hold["o"]
    with ExitStack() as c2:
        m = p.sb("l4m", [128, 2, D], F32, c2)
        gbc = p.sb("l4g", [128, D], F32, c2)
        p.junk = p.sb("l4j", [128, D], F32, c2)
        bt = p.barrier()
        gt = p.load("gbc", gbc[:, :], a["g_post11"], bt)
        p.x_t = p.out_post(a["nsa_out"], lt2, m, gbc[:, :], gt)


def build(nc, a, out, parts=("1", "2", "n", "3", "f0", "4", "f1")):
    with ExitStack() as ctx:
        p = Program(nc, ctx)
        p.cst_t = [p.load("cst", p.cst[:, :], a["cst"], eng=p.A), p.load("cst", p.col[:, :], a["col"], eng=p.A)]
        p.x_t = [p.load("x", p.x[:, :, :], a["x"][0].rearrange("(t p) d -> p t d", p=128), eng=p.A)]
        for e in (p.V, p.A, p.P):
            e.wait(p.cst_t)
        for part in parts:
            {"1": layer1, "2": layer2, "n": final_first, "3": layer3, "4": layer4,
             "f0": lambda p, a: p.ffn(a, 0, "a"), "f1": lambda p, a: p.ffn(a, 1, "b")}[part](p, a)
        t = p.load("out", out[0].rearrange("(t p) d -> p t d", p=128), p.x[:, :, :], p.x_t, eng=p.S)
        p.S.wait(t)
        block = ctx.enter_context(nc.Block())

        def play(engine):
            def run(e):
                for f in engine.list:
                    f(e)
            return run

        block.sync(play(p.S))
        block.scalar(play(p.A))
        block.vector(play(p.V))
        block.gpsimd(play(p.G))
        block.tensor(play(p.P))


def arrange(i):
    def tiles(w, cols=None):
        k, n = w.shape
        return np.ascontiguousarray(w.reshape(k // 512, 4, 128, n // 512, 512).transpose(3, 0, 2, 1, 4)
                                    .reshape(-1, 128, TILE))

    def small(w):
        return np.ascontiguousarray(w.reshape(16, 128, -1).transpose(1, 0, 2).reshape(128, -1))

    def cols(v):
        return v.reshape(-1, 128).T

    def rows(v):
        return np.ascontiguousarray(np.broadcast_to(v.reshape(1, -1), (128, v.size)))

    f = {k: np.asarray(v) for k, v in i.items()}
    d = {"x": f["x"], "cst": constants(), "dist": distances()}
    dist = d["dist"]
    d["dist4"] = np.ascontiguousarray(dist[:, M_C:M_N])
    ev = f["ev_w_in"][0]
    d["ev_in"] = tiles(ev)
    d["ev_out"] = tiles(f["ev_w_out"][0])
    d["ev_wa"] = np.ascontiguousarray(f["ev_w_a"][0].transpose(1, 0, 2).reshape(128, -1))
    d["ev_wi"] = np.ascontiguousarray(f["ev_w_i"][0].transpose(1, 0, 2).reshape(128, -1))
    od = f["od_w_in"][0]
    d["od_in"] = tiles(np.concatenate([od[:, 0:2048], od[:, 2064:6160]], axis=1))
    d["od_alr"] = small(od[:, 2048:2064])
    d["od_out"] = tiles(f["od_w_out"][0])
    d["w_alpha"] = f["od_w_alpha"][0]
    d["head_norm"] = rows(f["od_head_norm"][0])
    d["v_norm"] = rows(f["od_v_norm"][0])
    d["w_s"] = np.ascontiguousarray(f["od_w_s"][0].transpose(2, 0, 1).reshape(128, -1))
    d["final_norm"] = rows(f["final_norm"])
    ab = f["ab_w_in_2"][0]
    d["ab_in"] = tiles(ab[:, 0:8192])
    d["ab_small"] = small(ab[:, 8192:8208])
    d["ab_out"] = tiles(f["ab_w_out_2"][0])
    d["gn3"] = rows(np.concatenate([f["hgrn_norm_g_2"][0], f["gdn_norm_g_2"][0]]))
    ns = f["nsa_w_in_2"][0]
    d["nsa_in"] = tiles(ns[:, 0:5120])
    d["nsa_small"] = small(ns[:, 5120:5168])
    d["nsa_out"] = tiles(f["nsa_w_out_2"][0])
    d["cmp_w1"] = np.ascontiguousarray(f["nsa_cmp_w1_2"][0].reshape(2, 2, 16, 128, 128).transpose(0, 1, 3, 2, 4)
                                       .reshape(4, 128, TILE))
    d["cmp_w2"] = np.ascontiguousarray(f["nsa_cmp_w2_2"][0].transpose(1, 0, 2).reshape(128, -1))
    d["ffn_gu"] = np.stack([tiles(f["ffn_w_gu_2"][l]) for l in range(2)])
    d["ffn_down"] = np.stack([tiles(f["ffn_w_down_2"][l]) for l in range(2)])
    for l in range(2):
        for n in (1, 3):
            d[f"g_post{l}{n}"] = rows(f["norm_g_2"][l, n])
    c = {"ev_norm": cols(f["ev_norm"][0]), "ev_conv_w": cols(f["ev_conv_w"][0]), "ev_conv_b": cols(f["ev_conv_b"][0]),
         "ev_b_a": cols(f["ev_b_a"][0]), "ev_b_i": cols(f["ev_b_i"][0]), "ev_lam": cols(f["ev_lam"][0]),
         "od_norm": cols(f["od_norm"][0]), "od_b_alpha": cols(f["od_b_alpha"][0]), "od_b_s": cols(f["od_b_s"][0]),
         "norm00": cols(f["norm_g_2"][0, 0]), "norm02": cols(f["norm_g_2"][0, 2]),
         "norm10": cols(f["norm_g_2"][1, 0]), "norm12": cols(f["norm_g_2"][1, 2]),
         "gdn_conv": cols(f["gdn_conv_w_2"][0]), "lb": cols(f["hgrn_lb_logits_2"][0]),
         "a_log": rows(f["gdn_a_log_2"][0]), "dt_bias": rows(f["gdn_dt_bias_2"][0]),
         "pos0": f["nsa_cmp_pos_2"][0, 0].T, "pos1": f["nsa_cmp_pos_2"][0, 1].T}
    d["col"] = np.ascontiguousarray(np.concatenate([c[k] for k, _ in COLS], axis=1))
    return d


def kernel(**inputs):
    import concourse.bacc as _bacc
    from concourse.bass_utils import run_bass_kernel_spmd as _run

    nc = _bacc.Bacc("TRN2", target_bir_lowering=False, num_devices=1)
    arrays, a = {}, {}
    for name, v in arrange(inputs).items():
        arrays["in_" + name] = v
        a[name] = nc.dram_tensor("in_" + name, v.shape, mybir.dt.from_np(v.dtype), kind="ExternalInput").ap()
    out = nc.dram_tensor("out_y", (1, 256, D), F32, kind="ExternalOutput").ap()
    build(nc, a, out)
    r = _run(nc, [arrays], core_ids=[0])
    return r.results[0]["out_y"]
```

```python
from contextlib import ExitStack

import numpy as np

import concourse.bass as bass
from concourse import mybir

F32 = mybir.dt.float32
F32R = mybir.dt.float32r
I32 = mybir.dt.int32
ALU = mybir.AluOpType
ACT = mybir.ActivationFunctionType
AX = mybir.AxisListType
MUL, ADD, SUB, MAX, MIN = ALU.mult, ALU.add, ALU.subtract, ALU.max, ALU.min

D = 2048
EPS = 1e-6
SQ = 128.0 ** -0.5
NRAW = 3
NSPLIT = 5
R1 = ((1, 2), (1, 1), (1, 1))
R4 = ((7, 5), (4, 3))
R3 = ((5, 3), (4, 3), (6, 5))
TILE = 2048
HALF = 1024
LNEXP = "natural_log_exp_and_others"

C_ID = 0
C_ZERO = 128
C_TRI = 256
C_ONE = 384
C_LEV = 512
C_EPS = C_LEV + 7 * 128
C_HALF = C_EPS + 1
C_N = C_HALF + 8

COLS = [("ev_norm", 16), ("ev_conv_w", 48), ("ev_conv_b", 12), ("ev_b_a", 12), ("ev_b_i", 12), ("ev_lam", 12),
        ("od_norm", 16), ("od_b_alpha", 4), ("od_b_s", 4), ("norm00", 16), ("norm02", 16), ("norm10", 16),
        ("norm12", 16), ("gdn_conv", 96), ("lb", 8), ("a_log", 8), ("dt_bias", 8), ("pos0", 32), ("pos1", 32)]
COL_AT = {}
_n = 0
for _k, _w in COLS:
    COL_AT[_k] = (_n, _w)
    _n += _w
COL_N = _n

M_G = [0, 384, 768]
M_C = 1152
M_CMP = 1536
M_VAL = M_CMP + 32
M_N = M_VAL + 32

SLOPE = [[2.0 ** (-8.0 * (g + 3 * j + 1) / 12) for j in range(4)] for g in range(3)]
SLOPE2 = [2.0 ** (-8.0 * (h + 1) / 16) for h in range(16)]


def constants():
    s = np.arange(128)[:, None]
    t = np.arange(128)[None, :]
    parts = [np.eye(128), np.zeros((128, 128)), s <= t, np.ones((128, 128))]
    for level in range(7):
        h = 1 << level
        parts.append((s // (2 * h) == t // (2 * h)) & (s % (2 * h) < h) & (t % (2 * h) >= h))
    parts.append(np.full((128, 1), EPS))
    parts.append(np.full((128, 8), -0.5))
    return np.concatenate([np.asarray(x, np.float32) for x in parts], axis=1)


def distances():
    out = []
    big = 1e32
    for dil, most in ((1, 128), (4, 512), (16, 2048), (1, 512)):
        for base, n in ((0, 128), (128, 256)):
            d = base + np.arange(128)[:, None] - np.arange(n)[None, :]
            ok = (d >= 0) & (d <= most) & (d % dil == 0)
            out.append(np.where(ok, d, big))
    for keep in (False, True):
        for base in (0, 128):
            d = base + np.arange(128)[:, None] - (16 * np.arange(15)[None, :] + 31)
            v = (d >= 0) if keep else np.where(d >= 0, d, big)
            out += [v, np.zeros((128, 1))]
    return np.concatenate([np.asarray(x, np.float32) for x in out], axis=1)


class Engine:

    def __init__(self, sem):
        self.sem = sem
        self.list = []
        self.n = 0
        self.past = {}

    def wait(self, *toks):
        for t in toks:
            if t is None:
                continue
            if isinstance(t, list):
                self.wait(*t)
                continue
            sem, v = t
            if self.past.get(id(sem), 0) < v:
                self.past[id(sem)] = v
                self.list.append(lambda e, sem=sem, v=v: e.wait_ge(sem, v))

    def do(self, fn, *toks, sig=True):
        self.wait(*toks)
        if not sig:
            self.list.append(fn)
            return None
        self.n += 1
        self.list.append(lambda e: fn(e).then_inc(self.sem, 1))
        return (self.sem, self.n)

    def now(self):
        return (self.sem, self.n)

    def dma(self, out, in_, sem, *toks):
        self.wait(*toks)
        self.list.append(lambda e: e.dma_start(out, in_).then_inc(sem[0], 16))
        sem[1] += 16
        return (sem[0], sem[1])

    def tt(self, out, a, b, op, *w):
        return self.do(lambda e: e.tensor_tensor(out, a, b, op), *w)

    def ts(self, out, a, s1, s2, op0, op1, *w):
        if op1 is None:
            return self.do(lambda e: e.tensor_scalar(out, a, s1, None, op0), *w)
        return self.do(lambda e: e.tensor_scalar(out, a, s1, s2, op0, op1), *w)

    def stt(self, out, a, s, b, op0, op1, *w):
        return self.do(lambda e: e.scalar_tensor_tensor(out=out, in0=a, scalar=s, in1=b, op0=op0, op1=op1), *w)

    def cp(self, out, a, *w):
        return self.do(lambda e: e.tensor_copy(out, a), *w)

    def rec(self, out, a, *w):
        return self.do(lambda e: e.reciprocal(out, a), *w)

    def red(self, out, a, op, *w):
        return self.do(lambda e: e.tensor_reduce(out, a, AX.X, op), *w)

    def pred(self, out, mask, a, *w):
        return self.do(lambda e: e.copy_predicated(out, mask, a), *w)

    def act(self, out, a, func, *w, bias=None, scale=None, acc=None):
        kw = {}
        if bias is not None:
            kw["bias"] = bias
        if scale is not None:
            kw["scale"] = scale
        if acc is not None:
            kw["accum_out"] = acc
        return self.do(lambda e: e.activation(out, a, func, **kw), *w)

    def mm(self, out, l, r, *w, start=True, stop=True, sig=False):
        return self.do(lambda e: e.matmul(out, l, r, start=start, stop=stop, skip_group_check=True), *w, sig=sig)

    def tr(self, out, a, ident, *w, sig=False):
        return self.do(lambda e: e.transpose(out, a, ident), *w, sig=sig)


class Slot:
    def __init__(self, t):
        self.t = t
        self.free = []
        self.held = False

    def done(self, *toks):
        assert self.held
        self.free = list(toks)
        self.held = False


class Ring:

    def __init__(self, items):
        self.slots = [Slot(x) for x in items]
        self.i = 0

    def get(self):
        s = self.slots[self.i % len(self.slots)]
        self.i += 1
        assert not s.held
        s.held = True
        return s


def bc(ap, shape):
    return ap.to_broadcast(shape)


class Program:
    def __init__(self, nc, ctx, a, sched):
        self.nc = nc
        self.ctx = ctx
        self.a = a
        sem = lambda n: ctx.enter_context(nc.semaphore(n))
        self.sem = sem
        self.V, self.A, self.P, self.G, self.S = (Engine(sem("s_" + n)) for n in ("dve", "act", "pe", "pool", "sp"))
        self.ws = [[sem(f"s_w{i}"), 0] for i in range(NRAW)]
        self.ls = {}
        sb = self.sb
        self.raw = Ring([sb(f"raw{i}", [128, TILE])[:, :] for i in range(NRAW)])
        self.hi = Ring([sb(f"whi{i}", [128, HALF], F32R)[:, :] for i in range(NSPLIT)])
        self.lo = Ring([sb(f"wlo{i}", [128, HALF], F32R)[:, :] for i in range(NSPLIT)])
        self.x = sb("xres", [128, 2, D])
        self.xhi = sb("xhi", [128, 16, 256], F32R)
        self.xlo = sb("xlo", [128, 16, 256], F32R)
        self.cst = sb("cst", [128, C_N])
        self.col = sb("col", [128, COL_N])
        self.st = sb("st", [128, 512])
        self.sq = sb("sq", [128, 512])
        self.st_i = 0
        banks = [ctx.enter_context(nc.psum_tensor(f"ps{i}", [128, 512], F32))[:, :] for i in range(8)]
        self.acc = Ring(banks[0:4])
        self.ps = Ring(banks[4:8])
        self.ident = self.cst[:, C_ID:C_ID + 128]
        self.sched = sched
        self.pieces = []
        self.used = 0
        self.bgs = []
        self.rate = (1, 1)
        self.dg_t = None
        self.beat = 0
        self.ss = None
        self.xt = {0: [], 1: []}

    def sb(self, name, shape, dt=F32, ctx=None):
        return (ctx or self.ctx).enter_context(self.nc.sbuf_tensor(name, shape, dt))

    def load(self, name, out, in_, *w, eng=None):
        if name not in self.ls:
            self.ls[name] = [self.sem("s_l_" + name), 0]
        return (eng or self.G).dma(out, in_, self.ls[name], *w)

    def c(self, name, i=0, n=1):
        a, w = COL_AT[name]
        return self.col[:, a + i:a + i + n]

    def cell(self, n=1):
        if self.st_i + n > 512:
            self.st_i = 0
        a = self.st_i
        self.st_i += n
        return self.st[:, a:a + n]

    def barrier(self):
        if self.ss:
            self.next_rstd = self.rstd()
        now = [e.now() for e in (self.V, self.A, self.P, self.G)]
        for e in (self.V, self.A, self.P, self.G):
            e.wait(now)
        return now

    def bg(self, gen, rate=(1, 1)):
        self.bgs.append(gen)
        self.rate = rate

    def step(self):
        if self.bgs:
            try:
                next(self.bgs[0])
            except StopIteration:
                self.bgs.pop(0)

    def tick(self):
        n, d = self.rate
        self.beat += n
        while self.beat >= d:
            self.beat -= d
            self.step()

    def finish(self):
        while self.bgs:
            self.step()

    def feed(self):
        name, ti, off, n, total = self.sched[len(self.pieces)]
        if off == 0:
            s = self.raw.get()
            k = (self.raw.i - 1) % NRAW
            src = self.a[name] if ti is None else self.a[name][ti]
            self.now_raw = s, self.S.dma(s.t[:, 0:total], src, self.ws[k], s.free)
        s, tok = self.now_raw
        h, l = self.hi.get(), self.lo.get()
        r = s.t[:, off:off + n]
        th = self.A.act(h.t[:, 0:n], r, ACT.Copy, tok, h.free)
        tl = self.V.tt(l.t[:, 0:n], r, h.t[:, 0:n].bitcast(F32), SUB, tok, th, l.free)
        if off + n == total:
            s.done(th, tl)
        h.held = l.held = False
        self.pieces.append((h, l, tl))

    def ahead(self):
        while len(self.pieces) < min(self.used + NSPLIT - 1, len(self.sched)):
            self.feed()

    def take(self, name, ti, off):
        assert self.sched[self.used][0:3] == (name, ti, off), (self.sched[self.used], name, ti, off)
        self.ahead()
        h, l, tok = self.pieces[self.used]
        self.used += 1
        h.held = l.held = True
        return h, l, tok

    def proj(self, name, tiles, mode, lhs=None, lt=None, ks=None):
        P = self.P
        xhi, xlo = lhs or (self.xhi, self.xlo)
        b = [self.acc.get(), self.acc.get()]
        n = len(tiles)
        for i, ti in enumerate(tiles):
            for hf in range(2):
                h, l, tok = self.take(name, ti, hf * HALF)
                P.wait(tok)
                if i == 0 and hf == 0:
                    P.wait(b[0].free, b[1].free)
                for j in range(2):
                    k = 4 * (ks[i] if ks else i) + 2 * hf + j
                    P.wait(lt[k] if isinstance(lt, dict) else lt)
                    first, last = (i, hf, j) == (0, 0, 0), (i, hf, j) == (n - 1, 1, 1)
                    if mode == "A":
                        wh, wl = h.t[:, j * 512:(j + 1) * 512], l.t[:, j * 512:(j + 1) * 512]
                        for tt in range(2):
                            a, c = xhi[:, k, tt * 128:(tt + 1) * 128], xlo[:, k, tt * 128:(tt + 1) * 128]
                            P.mm(b[tt].t, a, wh, start=first, stop=False)
                            P.mm(b[tt].t, a, wl, start=False, stop=False)
                            t = P.mm(b[tt].t, c, wh, start=False, stop=last, sig=(j == 1 and tt == 1))
                    else:
                        for f in range(4):
                            o = j * 512 + f * 128
                            out = b[f // 2].t[:, (f % 2) * 256:(f % 2) * 256 + 256]
                            P.mm(out, h.t[:, o:o + 128], xhi[:, k, :], start=first and f % 2 == 0, stop=False)
                            P.mm(out, h.t[:, o:o + 128], xlo[:, k, :], start=False, stop=False)
                            t = P.mm(out, l.t[:, o:o + 128], xhi[:, k, :], start=False, stop=last,
                                     sig=(j == 1 and f == 3))
                h.done(t)
                l.done(t)
                self.tick()
        return b, t

    def proj_small(self, name, nc_, lt=None):
        P = self.P
        h, l, tok = self.take(name, None, 0)
        b = self.acc.get()
        other = self.acc.get()
        P.wait(tok, b.free, lt if not isinstance(lt, dict) else list(lt.values()))
        out = b.t[0:nc_, 0:256]
        for k in range(16):
            wh, wl = h.t[:, k * nc_:(k + 1) * nc_], l.t[:, k * nc_:(k + 1) * nc_]
            P.mm(out, wh, self.xhi[:, k, :], start=(k == 0), stop=False)
            P.mm(out, wh, self.xlo[:, k, :], start=False, stop=False)
            t = P.mm(out, wl, self.xhi[:, k, :], start=False, stop=(k == 15), sig=(k == 15))
        h.done(t)
        l.done(t)
        other.done(*other.free)
        return b, t

    def tokens_first(self, nc_, dst, tw, *w):
        P = self.P
        bk = self.ps.get()
        P.wait(bk.free, tw)
        for tt in range(2):
            t = P.tr(bk.t[:, tt * 64:tt * 64 + nc_], self.sq[0:nc_, tt * 128:(tt + 1) * 128],
                     self.ident[0:nc_, 0:nc_], sig=True)
        self.dg_t = t
        t = self.A.act(dst, bk.t[:, 0:128].rearrange("p (a n) -> p a n", a=2)[:, :, 0:nc_], ACT.Copy, t, *w)
        bk.done(t)
        return t

    def rsqrt(self, ss, n, scale, *w):
        v, r = self.cell(n), self.cell(n)
        t = self.V.ts(v, ss, scale, EPS, MUL, ADD, *w)
        return r, self.G.tt(r, v, self.cst[:, C_HALF:C_HALF + n], ALU.pow, t)

    def square(self, tt, nb, src, *w):
        if not self.ss:
            self.ss = {"c": self.cell(8), "t": []}
        c = self.ss["c"][:, 4 * tt + nb:4 * tt + nb + 1]
        self.ss["t"].append(self.A.act(self.sq[:, :], src, ACT.Square, *w, self.A.now(), self.dg_t, acc=c))

    def rstd(self):
        s = self.cell(2)
        t = self.V.red(s, self.ss["c"].rearrange("p (a n) -> p a n", a=2), ADD, self.ss["t"])
        self.ss = None
        return self.rsqrt(s, 2, 1.0 / D, t)

    def square_all(self):
        for nb in range(4):
            for tt in range(2):
                self.square(tt, nb, self.x[:, tt, nb * 512:(nb + 1) * 512], self.xt[tt][nb])

    def norm_T(self, gname):
        V, A, P = self.V, self.A, self.P
        r, t = self.next_rstd
        dg, td = [], []
        for tt in range(2):
            d = self.sq[:, tt * 128:(tt + 1) * 128]
            dg.append(d)
            td.append(V.ts(d, self.ident, r[:, tt:tt + 1], None, MUL, None, t, A.now()))
        self.ahead()
        out = {}
        hold = {}

        def turn(i):
            b = self.ps.get()
            P.wait(b.free, td, self.xt[0], self.xt[1])
            for j in range(2):
                for tt in range(2):
                    c = 2 * i + j
                    t = P.mm(b.t[:, j * 256 + tt * 128:j * 256 + tt * 128 + 128], self.x[:, tt, c * 128:(c + 1) * 128],
                             dg[tt], start=(j == 0 and tt == 0), sig=True)
            hold[i] = b, t

        def parts(i):
            b, t = hold[i]
            for c in (2 * i, 2 * i + 1):
                j = c % 2
                th = A.act(self.xhi[:, c, :], b.t[:, j * 256:(j + 1) * 256], ACT.Copy, t, scale=self.c(gname, c))
            for c in (2 * i, 2 * i + 1):
                j = c % 2
                tl = V.stt(self.xlo[:, c, :], b.t[:, j * 256:(j + 1) * 256], self.c(gname, c),
                           self.xhi[:, c, :].bitcast(F32), MUL, SUB, th)
                out[c] = [th, tl]
            b.done(tl)

        self.run(gskew(8, [turn, parts]))
        self.dg_t = self.P.now()
        return out

    def to_lhs(self, src, c, n, *w):
        th = self.A.act(self.xhi[:, c:c + n, :], src, ACT.Copy, *w)
        tl = self.V.tt(self.xlo[:, c:c + n, :], src, self.xhi[:, c:c + n, :].bitcast(F32), SUB, *w, th)
        return [th, tl]

    def turn(self, src, c0, nch, *w):
        P = self.P
        for c in range(0, nch, 2):
            b = self.ps.get()
            P.wait(b.free, *w)
            for i in range(2):
                for tt in range(2):
                    t = P.tr(b.t[:, i * 256 + tt * 128:i * 256 + tt * 128 + 128],
                             src[:, tt, (c + i) * 128:(c + i + 1) * 128], self.ident, sig=True)
            o = self.xhi[:, c0 + c:c0 + c + 2, :]
            p = b.t.rearrange("p (c n) -> p c n", c=2)
            th = self.A.act(o, p, ACT.Copy, t)
            tl = self.V.tt(self.xlo[:, c0 + c:c0 + c + 2, :], p, o.bitcast(F32), SUB, th)
            b.done(tl)
            self.turned = [th, tl]
            yield

    def run(self, gen):
        for _ in gen:
            pass

    def out_part(self, name, ks, lt, dst=None, last=False, first=True):
        for nb in range(4):
            b, t = self.proj(name, [nb * 4 + k for k in ks], "A", lt=lt, ks=ks)
            for tt in range(2):
                ns = slice(nb * 512, (nb + 1) * 512)
                if dst is None:
                    xs = self.x[:, tt, ns]
                    tv = self.V.tt(xs, b[tt].t, xs, ADD, t)
                    if last:
                        self.xt[tt] = (self.xt[tt] if nb else []) + [tv]
                else:
                    xs = dst[:, tt, ns]
                    if first:
                        tv = self.A.act(xs, b[tt].t, ACT.Copy, t)
                    else:
                        tv = self.V.tt(xs, b[tt].t, xs, ADD, t)
                b[tt].done(tv)
                if last:
                    self.square(tt, nb, xs, tv)
            if last and dst is not None:
                self.gain(dst, nb)

    def gain(self, m, nb):
        ns = slice(nb * 512, (nb + 1) * 512)
        squared = self.ss["t"][-2:]
        if nb == 3:
            self.m_rstd = self.rstd()
        for tt in range(2):
            self.mg = self.V.tt(m[:, tt, ns], m[:, tt, ns], self.gpost[:, ns], MUL, squared, self.tpost)

    def post(self, m, last=False):
        r, t = self.m_rstd
        self.xt = {0: [], 1: []}
        for nb in range(4):
            ns = slice(nb * 512, (nb + 1) * 512)
            for tt in range(2):
                xs = self.x[:, tt, ns]
                t1 = self.V.stt(xs, m[:, tt, ns], r[:, tt:tt + 1], xs, MUL, ADD, t, self.mg)
                self.xt[tt].append(t1)
                if not last:
                    self.square(tt, nb, xs, t1)

    def headnorm(self, o, nh, dv, gb, gate, sq, *w):
        V, A = self.V, self.A
        n = nh * dv
        rr = []
        for tt in range(2):
            s = sq[:, tt * n:(tt + 1) * n]
            t1 = A.act(s, o[:, tt, :], ACT.Square, *w)
            ss = self.cell(nh)
            t2 = V.red(ss, s.rearrange("p (h e) -> p h e", h=nh), ADD, t1)
            rr.append(self.rsqrt(ss, nh, 1.0 / dv, t2))
            yield
        out = []
        for tt in range(2):
            r, t3 = rr[tt]
            oo = o[:, tt, :].rearrange("p (h e) -> p h e", h=nh)
            t4 = V.tt(oo, oo, bc(r.unsqueeze(2), [128, nh, dv]), MUL, t3)
            if gb.shape[1] == n:
                t5 = V.tt(o[:, tt, :], o[:, tt, :], gb, MUL, t4, *w)
            else:
                t5 = V.tt(oo, oo, bc(gb.unsqueeze(1), [128, nh, dv]), MUL, t4, *w)
            yield
            out.append(V.tt(o[:, tt, :], o[:, tt, :], gate[:, tt, :], MUL, t5, *w))
            yield
        self.hn = out

    def ffn(self, layer, tag, last=False):
        V, A, P = self.V, self.A, self.P
        with ExitStack() as c:
            hh = self.sb("hh" + tag, [128, 24, 256], F32R, c)
            hl = self.sb("hl" + tag, [128, 24, 256], F32R, c)
            m = self.sb("fm" + tag, [128, 2, D], F32, c)
            gbc = self.sb("fg" + tag, [128, D], F32, c)
            tmp = Ring([self.sb(f"ft{tag}{i}", [128, 512], F32, c)[:, :] for i in range(4)])
            bt = self.barrier()
            self.gpost = gbc[:, :]
            self.tpost = self.load("gbc", gbc[:, :], self.a[f"g_post{layer}3"], bt)
            lt = self.norm_T(f"norm{layer}2")
            wgu, wd = f"ffn_gu{layer}", f"ffn_down{layer}"
            done = None
            hts = {}
            for half, blocks in enumerate((range(0, 6), range(6, 11))):
                for i, nb in enumerate(blocks):
                    bg, tg = self.proj(wgu, range(nb * 4, nb * 4 + 4), "B", lt=lt)
                    sg = []
                    for q in range(2):
                        s = tmp.get()
                        t1 = A.act(s.t, bg[q].t, ACT.Silu, tg, s.free)
                        bg[q].done(t1)
                        sg.append((s, t1))
                    bu, tu = self.proj(wgu, range((11 + nb) * 4, (11 + nb) * 4 + 4), "B", lt=lt)
                    for q in range(2):
                        s, t1 = sg[q]
                        t2 = V.tt(s.t, s.t, bu[q].t, MUL, tu, t1)
                        bu[q].done(t2)
                        k = i * 4 + q * 2
                        s3 = s.t.rearrange("p (c n) -> p c n", c=2)
                        t3 = A.act(hh[:, k:k + 2, :], s3, ACT.Copy, t2, done)
                        t4 = V.tt(hl[:, k:k + 2, :], s3, hh[:, k:k + 2, :].bitcast(F32), SUB, t3, done)
                        s.done(t3, t4)
                        ht = [t3, t4]
                        hts[k] = hts[k + 1] = ht
                n = len(blocks)
                for nb in range(4):
                    b, t = self.proj(wd, range(nb * 11 + half * 6, nb * 11 + half * 6 + n), "A", (hh, hl), hts)
                    ns = slice(nb * 512, (nb + 1) * 512)
                    for tt in range(2):
                        ms = m[:, tt, ns]
                        if half == 0:
                            tm = A.act(ms, b[tt].t, ACT.Copy, t, V.now())
                            b[tt].done(tm)
                        else:
                            tm = V.tt(ms, ms, b[tt].t, ADD, t, A.now())
                            b[tt].done(tm)
                            self.square(tt, nb, ms, tm)
                    if half:
                        self.gain(m, nb)
                done = [t]
            self.post(m, last)

    def decay_attention(self, q, k, b, v, o, nh, dv, E, At, Ac, rt):
        V, A, P = self.V, self.A, self.P
        nI = nh * 2
        lev = lambda l: self.cst[:, C_LEV + l * 128:C_LEV + (l + 1) * 128]
        t0 = V.do(lambda e: e.memset(At[:, 0:nI * 128], 0.0), rt)
        ring = Ring(E)
        hold = {}

        def inst(ap, i):
            return ap[:, i * 128:(i + 1) * 128]

        def prepare(it):
            if it == 0:
                return
            h = 1 << (it - 1)
            sl = ring.get()
            X = sl.t
            r3 = lambda ap: ap.rearrange("p (m n) -> p m n", n=2 * h)
            B, X3 = r3(b), r3(X)
            m = nh * 256 // (2 * h)
            ref = bc(B[:, :, h - 1:h], [128, m, h])
            t1 = V.tt(X3[:, :, 0:h], ref, B[:, :, 0:h], SUB, rt, sl.free)
            t2 = V.tt(X3[:, :, h:2 * h], B[:, :, h:2 * h], ref, SUB, rt, sl.free)
            hold[it] = sl, A.act(X, X, ACT.Exp, t1, t2)

        def scaled(it):
            if it:
                h = 1 << (it - 1)
                sl, t3 = hold[it]
                r3 = lambda ap: ap.rearrange("p (m n) -> p m n", n=2 * h)
                X3, K, Q = r3(sl.t), r3(k), r3(q)
                t4 = V.tt(X3[:, :, 0:h], X3[:, :, 0:h], K[:, :, 0:h], MUL, t3)
                t5 = V.tt(X3[:, :, h:2 * h], X3[:, :, h:2 * h], Q[:, :, h:2 * h], MUL, t3)
                hold[it] = sl, [t4, t5]

        def products(it):
            if it == 0:
                lhs, rhs, w = k, q, rt
            else:
                sl, w = hold[it]
                lhs = rhs = sl.t
            banks = []
            if it < 8:
                for g in range(0, nI, 4):
                    bk = self.ps.get()
                    P.wait(bk.free, w)
                    for i in range(4):
                        t = P.mm(bk.t[:, i * 128:(i + 1) * 128], inst(lhs, g + i), inst(rhs, g + i),
                                 start=(i == 0), sig=True)
                    banks.append((bk, t))
            else:
                for g in range(0, nh, 4):
                    bk = self.ps.get()
                    P.wait(bk.free, w)
                    for i in range(4):
                        t = P.mm(bk.t[:, i * 128:(i + 1) * 128], inst(lhs, 2 * (g + i)), inst(lhs, 2 * (g + i) + 1),
                                 start=(i == 0), sig=True)
                    banks.append((bk, t))
            if it:
                sl.done(t)
            hold[it] = banks

        def place(it):
            m = self.ident if it == 0 else (lev(it - 1) if it < 8 else None)
            for g, (bk, t) in enumerate(hold[it]):
                if it < 8:
                    tv = V.pred(At[:, g * 512:(g + 1) * 512].rearrange("p (i t) -> p i t", i=4),
                                bc(m.bitcast(I32).unsqueeze(1), [128, 4, 128]),
                                bk.t.rearrange("p (i t) -> p i t", i=4), t, hold.get(("a", g), t0))
                    hold["a"] = hold["a", g] = tv
                else:
                    tv = A.act(Ac[:, g * 512:(g + 1) * 512], bk.t, ACT.Copy, t)
                    hold["c"] = tv
                bk.done(tv)

        yield from gskew(9, [prepare, scaled, products, place])
        per = 512 // dv
        for tt in range(2):
            for g in range(0, nh, per):
                bk = self.ps.get()
                P.wait(bk.free, hold["a"], hold["c"])
                for i in range(per):
                    hd = g + i
                    out = bk.t[:, i * dv:(i + 1) * dv]
                    vv = lambda x: v[:, x, hd * dv:(hd + 1) * dv]
                    t = P.mm(out, inst(At, hd * 2 + tt), vv(tt), start=(i == 0), stop=(tt == 0), sig=True)
                    if tt == 1:
                        t = P.mm(out, inst(Ac, hd), vv(0), start=False, sig=True)
                yield
                self.da = A.act(o[:, tt, g * dv:(g + per) * dv], bk.t, ACT.Copy, t)
                bk.done(self.da)


def gskew(n, stages):
    m = len(stages)
    for t in range(n + m - 1):
        for s in reversed(range(m)):
            if 0 <= t - s < n:
                stages[s](t - s)
        yield


def inst_at(ap, i):
    return ap[:, i * 128:(i + 1) * 128]


def view2(b):
    return b.t.rearrange("p (c n) -> p c n", c=2)


def layer1(p):
    V, A, P, G, a = p.V, p.A, p.P, p.G, p.a
    with ExitStack() as c:
        sb = lambda n, s: p.sb("l1" + n, s, F32, c)
        xa = sb("xa", [128, 12, 260])
        xc = sb("xc", [128, 12, 256])
        RI = sb("ri", [128, 24, 256])
        R, I = RI[:, 0:12, :], RI[:, 12:24, :]
        ga = sb("ga", [128, 12, 256])
        vt = sb("vt", [128, 2, 1536])
        gb = sb("gb", [128, 4, 256])
        big = sb("mb", [128, 1024])
        dm = xa[:, :, :].rearrange("p c n -> p (c n)")
        wai = vt[:, :, :]
        bt = p.barrier()
        twa = p.load("wa", wai[:, 0, :], a["ev_wa"], bt)
        twi = p.load("wa", wai[:, 1, :], a["ev_wi"], bt)
        lt = p.norm_T("ev_norm")
        tz = V.do(lambda e: e.memset(xa[:, :, 0:3], 0.0))
        txa = {}
        for nb in range(3):
            b, t = p.proj("ev_in", range(nb * 4, nb * 4 + 4), "B", lt=lt)
            for q in range(2):
                k = nb * 4 + q * 2
                txa[k] = txa[k + 1] = A.act(xa[:, k:k + 2, 3:259], view2(b[q]), ACT.Copy, t)
                b[q].done(txa[k])
        lam = p.c("ev_lam", 0, 12)
        c8, s1, s2 = p.cell(12), p.cell(12), p.cell(12)
        A.do(lambda e: e.preload_act_table_set(LNEXP), sig=False)
        t1 = V.stt(s1, lam, -1.0, lam, MUL, MAX, p.cst_t)
        t2 = A.act(s1, s1, ACT.Exp, t1, scale=-1.0)
        t3 = A.act(s1, s1, ACT.Ln, t2, bias=1.0)
        t4 = V.ts(s2, lam, -1.0, 0.0, MUL, MAX, t1)
        t5 = V.tt(s2, s1, s2, ADD, t3, t4)
        tc8 = V.ts(c8, s2, -8.0, None, MUL, None, t5)
        TH = xa
        f = {}

        def lru():
            hold = {}

            def conv(ch):
                o = xc[:, ch, :]
                z = lambda j: xa[:, ch, j:j + 256]
                cw = lambda j: p.c("ev_conv_w", j * 12 + ch)
                t = V.ts(o, z(0), cw(0), p.c("ev_conv_b", ch), MUL, ADD, txa[ch], tz)
                for j in range(1, 4):
                    t = V.stt(o, z(j), cw(j), o, MUL, ADD, t)
                hold[ch] = t

            def gate(ch):
                o = xc[:, ch, :]
                bk = p.ps.get()
                P.mm(bk.t[:, 0:256], wai[:, 0, ch * 128:(ch + 1) * 128], o, bk.free, hold[ch], twa, twi)
                t2 = P.mm(bk.t[:, 256:512], wai[:, 1, ch * 128:(ch + 1) * 128], o, start=False, sig=True)
                hold[ch] = bk, t2
                f["wa"] = t2

            def sig(ch):
                bk, t2 = hold[ch]
                tr = A.act(R[:, ch, :], bk.t[:, 0:256], ACT.Sigmoid, t2, bias=p.c("ev_b_a", ch))
                t3 = A.act(I[:, ch, :], bk.t[:, 256:512], ACT.Sigmoid, bias=p.c("ev_b_i", ch))
                bk.done(t3)
                A.act(TH[:, ch, 0:256], R[:, ch, :], ACT.Tanh, tr, tc8, V.now(), scale=c8[:, ch:ch + 1])
                f["u"] = V.tt(I[:, ch, :], I[:, ch, :], xc[:, ch, :], MUL, t3)

            yield from gskew(12, [conv, gate, sig])
            f["sig"] = A.now()
            yield
            A.do(lambda e: e.preload_act_table_set(LNEXP), sig=False)
            for g in range(3):
                th = TH[:, 4 * g:4 * g + 4, 0:256]
                m4 = big[:, :].rearrange("p (c n) -> p c n", c=4)
                t1 = A.act(m4, th, ACT.Ln, f["sig"], V.now(), scale=-1.0, bias=1.0)
                t2 = V.ts(th, th, -2.0, 1e-18, MUL, MAX, t1)
                for ch in range(4 * g, 4 * g + 4):
                    ta = A.act(R[:, ch, :], R[:, ch, :], ACT.Exp, f["sig"], scale=c8[:, ch:ch + 1])
                    if ch % 4 == 1:
                        yield
                yield
                t3 = A.act(th, th, ACT.Ln, t2)
                yield
                t4 = V.tt(th, th, m4, SUB, t3)
                t5 = A.act(th, th, ACT.Exp, t4, scale=0.5)
                yield
                tu = V.tt(I[:, 4 * g:4 * g + 4, :], I[:, 4 * g:4 * g + 4, :], th, MUL, t5, f["u"])
                for ch in range(4 * g, 4 * g + 4):
                    ts_ = V.do(lambda e, ch=ch: e.tensor_tensor_scan(xc[:, ch, :], R[:, ch, :], I[:, ch, :], 0.0,
                                                                    MUL, ADD), ta, tu)
                    if ch % 4 == 1:
                        yield
                yield
                f["y"] = V.tt(xc[:, 4 * g:4 * g + 4, :], xc[:, 4 * g:4 * g + 4, :], ga[:, 4 * g:4 * g + 4, :], MUL,
                              ts_, f["ga", g])
                yield

        def silu_blocks(i0, n, dst, key):
            for nb in range(n):
                b, t = p.proj("ev_in", range((i0 + nb) * 4, (i0 + nb) * 4 + 4), "B")
                for q in range(2):
                    k = nb * 4 + q * 2
                    d = dst[:, k:k + 2, :]
                    t1 = A.act(d, view2(b[q]), ACT.Sigmoid, t)
                    f[key, nb] = V.tt(d, d, view2(b[q]), MUL, t1)
                    b[q].done(f[key, nb])

        p.bg(lru(), R1[0])
        silu_blocks(3, 3, ga, "ga")
        p.rate = R1[1]
        silu_blocks(15, 1, gb, "gb")
        b0 = None
        for nb in range(3):
            b, t = p.proj("ev_in", range((12 + nb) * 4, (12 + nb) * 4 + 4), "A")
            for tt in range(2):
                tvv = A.act(vt[:, tt, nb * 512:(nb + 1) * 512], b[tt].t, ACT.Copy, t, f["wa"])
                b[tt].done(tvv)
        p.finish()
        ty = f["y"]
        tdm = p.load("dm", dm[:, 0:M_N], a["dist"], ty)
        for which, dst in ((0, R), (1, I)):
            for nb in range(3):
                i0 = 6 + 3 * which + nb
                b, t = p.proj("ev_in", range(i0 * 4, i0 * 4 + 4), "B")
                for q in range(2):
                    k = nb * 4 + q * 2
                    tq = A.act(dst[:, k:k + 2, :], view2(b[q]), ACT.Copy, t, ty, scale=SQ if which == 0 else 1.0)
                    b[q].done(tq)
        tproj = t
        to1 = {}
        for k in range(0, 12, 2):
            tk = p.to_lhs(xc[:, k:k + 2, :], k, 2, tproj, ty)
            to1[k] = to1[k + 1] = tk
        SR = Ring([ga[:, 3 * i:3 * i + 3, :].rearrange("p c n -> p (c n)") for i in range(4)])
        PT = Ring([dm[:, M_N:M_N + 768], big[:, 0:768]])
        hold = {}

        def scores(it):
            j, qt = it // 2, it % 2
            nk = 128 * (qt + 1)
            off = 128 * qt
            b0, b1 = p.ps.get(), p.ps.get()
            P.wait(b0.free, b1.free, tq)
            for g in range(3):
                bk, o = (b0, g * 256) if g < 2 else (b1, 0)
                t = P.mm(bk.t[:, o:o + nk], R[:, g * 4 + j, off:off + 128], I[:, g * 4 + j, 0:nk],
                         start=(g != 1), sig=True)
            hold[it] = b0, b1, t

        def soft(it):
            j, qt = it // 2, it % 2
            nk = 128 * (qt + 1)
            b0, b1, t = hold[it]
            s = SR.get()
            ts = []
            for g in range(3):
                bk, o = (b0, g * 256) if g < 2 else (b1, 0)
                mo = M_G[g] + (128 if qt else 0)
                ts.append(V.stt(s.t[:, g * nk:(g + 1) * nk], dm[:, mo:mo + nk], -SLOPE[g][j],
                                bk.t[:, o:o + nk], MUL, ADD, t, tdm, s.free, ty))
            b0.done(ts[1])
            b1.done(ts[2])
            mx, nm, den = p.cell(), p.cell(), p.cell()
            t1 = V.red(mx, s.t[:, 0:3 * nk], MAX, ts)
            t2 = V.ts(nm, mx, -1.0, None, MUL, None, t1)
            t3 = A.act(s.t[:, 0:3 * nk], s.t[:, 0:3 * nk], ACT.Exp, t2, bias=nm, acc=den)
            hold[it] = s, den, t3

        def scaled(it):
            qt = it % 2
            nk = 128 * (qt + 1)
            s, den, t3 = hold[it]
            rd = p.cell()
            t4 = V.rec(rd, den, t3)
            t5 = V.ts(s.t[:, 0:3 * nk], s.t[:, 0:3 * nk], rd, None, MUL, None, t4)
            hold[it] = s, t5

        def turn_p(it):
            s, t5 = hold[it]
            n = 3 * (it % 2 + 1)
            b0 = p.ps.get()
            b1 = p.ps.get() if n > 4 else None
            P.wait(b0.free, t5, b1.free if b1 else None)
            for i in range(n):
                bk = b0 if i < 4 else b1
                t = P.tr(bk.t[:, (i % 4) * 128:(i % 4) * 128 + 128], s.t[:, i * 128:(i + 1) * 128], p.ident, sig=True)
            s.done(t)
            hold[it] = b0, b1, n, t

        def moved(it):
            b0, b1, n, t = hold[it]
            pt = PT.get()
            m = min(n, 4)
            t6 = A.act(pt.t[:, 0:m * 128], b0.t[:, 0:m * 128], ACT.Copy, t, pt.free)
            b0.done(t6)
            if b1:
                t6 = A.act(pt.t[:, 512:n * 128], b1.t[:, 0:(n - 4) * 128], ACT.Copy)
                b1.done(t6)
            hold[it] = pt, t6

        def pv(it):
            j, qt = it // 2, it % 2
            kt = qt + 1
            pt, t6 = hold[it]
            bk = p.ps.get()
            P.wait(bk.free, t6, tvv)
            for g in range(3):
                for x in range(kt):
                    i = g * kt + x
                    hd = g * 4 + j
                    t = P.mm(bk.t[:, 0:128], vt[:, x, hd * 128:(hd + 1) * 128], pt.t[:, i * 128:(i + 1) * 128],
                             start=(i == 0), stop=(i == 3 * kt - 1), sig=True)
            pt.done(t)
            hold[it] = bk, t

        def gated(it):
            j, qt = it // 2, it % 2
            bk, t = hold[it]
            y = gb[:, j, qt * 128:(qt + 1) * 128]
            ty2 = V.tt(y, bk.t[:, 0:128], y, MUL, t, f["gb", 0])
            bk.done(ty2)
            if qt:
                to1[12 + j] = p.to_lhs(gb[:, j:j + 1, :], 12 + j, 1, ty2, tproj)

        def att():
            for t in range(8 * 2 + 5):
                for s_, fn in ((6, gated), (5, moved), (5, pv), (1, soft), (4, turn_p), (0, scores), (3, scaled)):
                    if (t - s_) % 2 == 0 and 0 <= (t - s_) // 2 < 8 and t >= s_:
                        fn((t - s_) // 2)
                yield

        p.bg(att(), R1[2])
        p.out_part("ev_out", [0, 1, 2], to1)
        p.finish()
        p.out_part("ev_out", [3], to1, last=True)


def layer2(p, final):
    V, A, P, G, a = p.V, p.A, p.P, p.G, p.a
    with ExitStack() as c:
        sb = lambda n, s: p.sb("l2" + n, s, F32, c)
        q = sb("q", [128, 1024])
        k = sb("k", [128, 1024])
        b_ = sb("b", [128, 1024])
        vt = sb("v", [128, 2, 1024])
        gc = sb("gc", [128, 2, 1024])
        u = sb("u", [128, 2, 1024])
        vd = sb("vd", [128, 2, 1024])
        gd = sb("gd", [128, 2, 1024])
        EE = sb("e", [128, 2, 1024])
        E1, E2 = EE[:, 0, :], EE[:, 1, :]
        At = sb("at", [128, 1024])
        Ac = sb("ac", [128, 512])
        hn = sb("hn", [128, 1024])
        vn = sb("vn", [128, 1024])
        W = sb("ws", [128, 512])
        E3 = sb("e3", [128, 1024])[:, :]
        bt = p.barrier()
        th = p.load("hn", hn[:, :], a["head_norm"], bt)
        tvn = p.load("vn", vn[:, :], a["v_norm"], bt)
        tws = p.load("ws", W[:, :], a["w_s"], bt)
        twal = p.load("wal", E2[0:16, 0:512], a["w_alpha"], bt)
        lt = p.norm_T("od_norm")
        f = {}

        def blk(i, mode):
            return p.proj("od_in", range(4 * i, 4 * i + 4), mode, lt=lt)

        for n, dst, sc in ((0, q, SQ), (1, k, 1.0)):
            b, t = blk(n, "B")
            for i in range(2):
                tq = A.act(dst[:, i * 512:(i + 1) * 512], b[i].t, ACT.Copy, t, scale=sc)
                b[i].done(tq)

        def tok(dst, i):
            for nb in range(2):
                b, t = blk(i + nb, "A")
                for tt in range(2):
                    te = A.act(dst[:, tt, nb * 512:(nb + 1) * 512], b[tt].t, ACT.Copy, t)
                    b[tt].done(te)
            return te

        bs, t = p.proj_small("od_alr", 16, lt)
        alT = E1[0:16, 0:256]
        ta = A.act(alT, bs.t[0:16, 0:256], ACT.Copy, t)
        bs.done(ta)

        def gla():
            bks = [p.ps.get(), p.ps.get()]
            P.wait(ta, twal, bks[0].free, bks[1].free)
            for h in range(4):
                t = P.mm(bks[h // 2].t[:, (h % 2) * 256:(h % 2) * 256 + 256], E2[0:16, h * 128:(h + 1) * 128], alT,
                         start=(h % 2 == 0), sig=True)
            yield
            for h in range(4):
                t3 = V.ts(b_[:, h * 256:(h + 1) * 256], bks[h // 2].t[:, (h % 2) * 256:(h % 2) * 256 + 256],
                          p.c("od_b_alpha", h), None, ADD, None, t)
            bks[0].done(t3)
            bks[1].done(t3)
            ab = At[:, :]
            t4 = V.stt(ab, b_[:, :], -1.0, b_[:, :], MUL, MAX, t3)
            yield
            A.do(lambda e: e.preload_act_table_set(LNEXP), sig=False)
            t5 = A.act(ab, ab, ACT.Exp, t4, scale=-1.0)
            t6 = A.act(ab, ab, ACT.Ln, t5, bias=1.0)
            yield
            t7 = V.stt(b_[:, :], b_[:, :], 0.0, ab, MIN, SUB, t6)
            t8 = V.ts(At[:, :], b_[:, :], 1.0 / 16.0, None, MUL, None, t7)
            yield
            for h in range(4):
                hs = slice(h * 256, (h + 1) * 256)
                t9 = V.do(lambda e, hs=hs: e.tensor_tensor_scan(b_[:, hs], At[:, hs], At[:, hs], 0.0, ADD,
                                                                ALU.bypass), t8)
            yield
            while "v" not in f:
                yield
            yield from p.decay_attention(q[:, :], k[:, :], b_[:, :], vt, EE, 4, 256, [E1, E2, E3], At, Ac,
                                         [t9, tq, t8, f["v"]])
            f["gla"] = p.da
            while "g" not in f:
                yield
            for tt in range(2):
                gs = A.act(gc[:, tt, :], gc[:, tt, :], ACT.Silu, f["g"])
            yield from p.headnorm(EE, 4, 256, hn[:, :], gc, Pair(q, k), f["gla"], th, gs)
            f["hn"] = p.hn
            while "vd" not in f:
                yield
            yield from gating()

        def gating():
            for tt in range(2):
                gv = A.act(vd[:, tt, :], vd[:, tt, :], ACT.Gelu_apprx_tanh, f["vd"])
            wsm = V.tt(W[:, :].rearrange("p (g t) -> p g t", g=4), W[:, :].rearrange("p (g t) -> p g t", g=4),
                       bc(p.cst[:, C_TRI:C_TRI + 128].unsqueeze(1), [128, 4, 128]), MUL, tws)
            rr = []
            for tt in range(2):
                z = vd[:, tt, :].rearrange("p (g e) -> p g e", g=4)
                mu, ss = p.cell(4), p.cell(4)
                t1 = V.red(mu, z, ADD, gv)
                t1 = V.ts(mu, mu, 1.0 / 256, None, MUL, None, t1)
                t2 = V.tt(z, z, bc(mu.unsqueeze(2), [128, 4, 256]), SUB, t1)
                rr.append((ss, A.act(vt[:, tt, :], vd[:, tt, :], ACT.Square, t2)))
                yield
            for tt in range(2):
                z = vd[:, tt, :].rearrange("p (g e) -> p g e", g=4)
                ss, t3 = rr[tt]
                t4 = V.red(ss, vt[:, tt, :].rearrange("p (g e) -> p g e", g=4), ADD, t3)
                r, t5 = p.rsqrt(ss, 4, 1.0 / 256, t4)
                yield
                t6 = V.tt(z, z, bc(r.unsqueeze(2), [128, 4, 256]), MUL, t5)
                f["vn", tt] = V.tt(vd[:, tt, :], vd[:, tt, :], vn[:, :], MUL, t6, tvn)
                yield
            while "gd" not in f:
                yield
            for tt in range(2):
                gu = A.act(u[:, tt, :], u[:, tt, :], ACT.Gelu_apprx_tanh, f["u"])
            for tt in range(2):
                gg = A.act(gd[:, tt, :], gd[:, tt, :], ACT.Silu, f["gd"])
            yield
            for tt in range(2):
                banks = []
                for g in range(0, 4, 2):
                    bk = p.ps.get()
                    P.wait(bk.free, f["vn", tt], wsm)
                    for i in range(2):
                        t = P.mm(bk.t[:, i * 256:(i + 1) * 256], W[:, (g + i) * 128:(g + i + 1) * 128],
                                 vd[:, tt, (g + i) * 256:(g + i + 1) * 256], start=(i == 0), sig=True)
                    banks.append((bk, t))
                ug = V.tt(u[:, tt, :], u[:, tt, :], gd[:, tt, :], MUL, gu, gg)
                yield
                for x, (bk, t) in enumerate(banks):
                    for i in range(2):
                        g = 2 * x + i
                        us = u[:, tt, g * 256:(g + 1) * 256]
                        tl = V.stt(us, bk.t[:, i * 256:(i + 1) * 256], p.c("od_b_s", g), us, ADD, MUL, t, ug)
                    bk.done(tl)
                yield
            yield from p.turn(u, 8, 8, tl, f["proj"])
            f["yd"] = p.turned

        p.bg(gla(), (2, 5))
        f["v"] = tok(vt, 2)
        f["vd"] = tok(vd, 8)
        f["g"] = tok(gc, 4)
        p.rate = (1, 1)
        f["u"] = tok(u, 6)
        tgd = tok(gd, 10)
        f["proj"] = P.now()
        while "hn" not in f:
            p.step()
        p.run(p.turn(EE, 0, 8, f["hn"], f["proj"]))
        yc = p.turned
        f["gd"] = tgd
        p.out_part("od_out", [0, 1], yc)
        p.finish()
        if final:
            g = vt[:, :, :].rearrange("p a n -> p (a n)")
            tg = p.load("fn", g, a["final_norm"], p.V.now(), p.P.now())
        p.out_part("od_out", [2, 3], f["yd"], last=True)
        if final:
            final_norm(p, g, tg)


class Pair:

    def __init__(self, a, b):
        self.t = (a, b)

    def __getitem__(self, key):
        s = key[1]
        i = s.start // 1024
        return self.t[i][:, s.start - 1024 * i:s.stop - 1024 * i]


def final_norm(p, g, tg):
    r, t = p.rstd()
    p.xt = {0: [], 1: []}
    for nb in range(4):
        ns = slice(nb * 512, (nb + 1) * 512)
        for tt in range(2):
            xs = p.x[:, tt, ns]
            t1 = p.V.stt(xs, xs, r[:, tt:tt + 1], g[:, ns], MUL, MUL, t, tg)
            p.square(tt, nb, xs, t1)
            p.xt[tt].append(t1)


def layer3(p):
    V, A, P, G, a = p.V, p.A, p.P, p.G, p.a
    with ExitStack() as c:
        ar = p.sb("l3", [128, 20800], F32, c)[:, :]
        at = [0]

        def take(n):
            o = at[0]
            at[0] += n
            assert at[0] <= 20800, at
            return ar[:, o:o + n]

        gn = take(256)
        sm = take(96).rearrange("p (a n) -> p a n", a=2)
        oall = take(4096)
        OA = [oall[:, i * 1024:(i + 1) * 1024].rearrange("p (a n) -> p a n", a=2) for i in range(4)]
        base = at[0]
        qk = take(2048).rearrange("p (c n) -> p c n", c=8)
        vb = take(1024).rearrange("p (a n) -> p a n", a=2)
        kb = take(1024)
        DT = take(1536)
        LT = take(1536)
        AT = take(1536)
        Tm = take(1024)
        Tt = take(1024)
        Mx = take(1024)
        vT = LT[:, 0:1024].rearrange("p (c n) -> p c n", c=4)
        zm = take(4096)
        Z = zm[:, 0:12 * 260].rearrange("p (c n) -> p c n", c=12)
        at[0] = base
        Kk, E1, E2, At = (take(1024) for _ in range(4))
        Ac = take(512)
        E3 = take(1024)
        at[0] = base + 8704
        QFV = [zm[:, 0:3072], take(3072)]
        Qs, Fs = ([QFV[g][:, i * 1024:(i + 1) * 1024] for g in range(2)] for i in range(2))
        Vs = [QFV[g][:, 2048:3072].rearrange("p (a n) -> p a n", a=2) for g in range(2)]
        m = zm.rearrange("p (a n) -> p a n", a=2)
        bt = p.barrier()
        tgn = p.load("gn", gn, a["gn3"], bt)
        lt = p.norm_T("norm00")
        f = {"hg": [P.now()]}
        lgt = p.c("lb", 0, 8)
        e1, e2, lb, oml = (p.cell(8) for _ in range(4))
        t = V.tt(e1, lgt, lgt, SUB, p.cst_t)
        t = A.act(e1, e1, ACT.Exp, t)
        t = V.rec(e2, e1, t)
        t = V.tt(e1, e1, e2, MUL, t)
        t = V.tt(lb, e1, e1, SUB, t)
        tlb = V.ts(oml, lb, -1.0, 1.0, MUL, ADD, t)

        def blkB(i, dst, z=None):
            b, t = p.proj("ab_in", range(i * 4, i * 4 + 4), "B", lt=lt)
            while z is not None and ("z", z) not in f:
                p.step()
            ww = [f["z", z] if z is not None else None]
            for h in range(2):
                te = A.act(dst[:, h * 512:(h + 1) * 512], b[h].t, ACT.Copy, t, *ww)
                b[h].done(te)
            return te

        def blkA(i, dst, z=None):
            b, t = p.proj("ab_in", range(i * 4, i * 4 + 4), "A", lt=lt)
            while z is not None and ("z", z) not in f:
                p.step()
            ww = [f["z", z] if z is not None else None]
            for tt in range(2):
                te = A.act(dst[:, tt, :], b[tt].t, ACT.Copy, t, *ww)
                b[tt].done(te)
            return te

        def hgrn(g, tq, tf, tv, tg):
            q, b_, vt, o = Qs[g], Fs[g], Vs[g], OA[g]
            prev = f["hg"]
            t1 = A.act(b_, b_, ACT.Sigmoid, tf)
            for h in range(4):
                s = slice(h * 256, (h + 1) * 256)
                hh = g * 4 + h
                t1 = V.ts(b_[:, s], b_[:, s], oml[:, hh:hh + 1], lb[:, hh:hh + 1], MUL, ADD, t1, tlb)
            yield
            t2 = V.ts(Kk, b_, -1.0, 1.0, MUL, ADD, t1, prev)
            t3 = V.ts(At, b_, 2.0 ** -63, None, MAX, None, t1, prev)
            A.do(lambda e: e.preload_act_table_set(LNEXP), sig=False)
            t4 = A.act(At, At, ACT.Ln, t3)
            yield
            for h in range(4):
                s = slice(h * 256, (h + 1) * 256)
                t9 = V.do(lambda e, s=s: e.tensor_tensor_scan(b_[:, s], At[:, s], At[:, s], 0.0, ADD, ALU.bypass),
                          t4, t2)
            yield
            oo = Kk.rearrange("p (a n) -> p a n", a=2)
            yield from p.decay_attention(q, Kk, b_, vt, oo, 4, 128, [E1, E2, E3], At, Ac, [t9, tq, tv, t4])
            for tt in range(2):
                t1 = A.act(o[:, tt, :], o[:, tt, :], ACT.Silu, tg)
            yield
            yield from p.headnorm(oo, 4, 128, gn[:, 0:128], o, E1, p.da, tgn)
            for tt in range(2):
                t1 = V.cp(o[:, tt, :], oo[:, tt, :], p.hn)
            f["oa", g] = t1
            f["hg"] = [V.now(), A.now(), P.now()]

        def conv(H, tz, parts=(0, 1, 2)):
            for part in parts:
                dst = qk[:, (0, 4)[part]:(0, 4)[part] + 4, :] if part < 2 else vT
                cw = lambda j, ch: p.c("gdn_conv", j * 24 + part * 8 + H * 4 + ch)
                zz = lambda j, ch: Z[:, part * 4 + ch, j:j + 256]
                for c0 in (0, 2):
                    ts_ = {}
                    for ch in (c0, c0 + 1):
                        ts_[ch] = A.act(dst[:, ch, :], zz(0, ch), ACT.Copy, tz, f["hg"], scale=cw(0, ch))
                    for j in range(1, 4):
                        for ch in (c0, c0 + 1):
                            d = dst[:, ch, :]
                            ts_[ch] = V.stt(d, zz(j, ch), cw(j, ch), d, MUL, ADD, ts_[ch])
                        if j == 2:
                            yield
                    f["conv"] = ts_[c0 + 1]
                    if c0:
                        f["z", part] = f["conv"]
                    yield

        def gdn(H, tz, tg, ts_):
            hd = H * 4
            prev = f["hg"]
            o = OA[2 + H]
            if H:
                yield from conv(1, tz)
            t = f["conv"]
            t1 = A.act(qk, qk, ACT.Silu, t)
            yield
            tsl = A.act(vT, vT, ACT.Silu, t)
            for tt in range(2):
                A.act(o[:, tt, :], o[:, tt, :], ACT.Silu, tg)
            tgs = A.now()
            yield
            tri = p.cst[:, C_TRI:C_TRI + 128]
            one = p.cst[:, C_ONE:C_ONE + 128]
            beta = lambda tt, h: sm[:, tt, 8 + h:9 + h]
            gcol = lambda tt, h: sm[:, tt, 24 + h:25 + h]
            if H == 0:
                bsv = sm[:, :, 32:48]
                ts_ = p.tokens_first(16, bsv, ts_)
                A.do(lambda e: e.preload_act_table_set(LNEXP), sig=False)
                ea = p.cell(8)
                te = A.act(ea, p.c("a_log", 0, 8), ACT.Exp)
                be = sm[:, :, 8:16]
                t2 = A.act(be, bsv[:, :, 8:16], ACT.Exp, ts_, scale=-1.0)
                t2 = V.ts(be, be, 1.0, None, ADD, None, t2)
                t2 = V.rec(be, be, t2)
                t1_ = V.tt(sm[:, :, 0:8], bsv[:, :, 0:8], bc(p.c("dt_bias", 0, 8).unsqueeze(1), [128, 2, 8]), ADD, ts_)
                t3 = V.stt(sm[:, :, 16:24], sm[:, :, 0:8], -1.0, sm[:, :, 0:8], MUL, MAX, t1_)
                t4 = A.act(sm[:, :, 16:24], sm[:, :, 16:24], ACT.Exp, t3, scale=-1.0)
                t5 = A.act(sm[:, :, 16:24], sm[:, :, 16:24], ACT.Ln, t4, bias=1.0)
                yield
                t6 = V.stt(sm[:, :, 0:8], sm[:, :, 0:8], 0.0, sm[:, :, 16:24], MAX, ADD, t5)
                t7 = V.tt(sm[:, :, 0:8], sm[:, :, 0:8], bc(ea.unsqueeze(1), [128, 2, 8]), MUL, t6, te)
                tld = V.ts(sm[:, :, 0:8], sm[:, :, 0:8], -1.0, None, MUL, None, t7)
                bk = p.ps.get()
                P.mm(bk.t[:, 0:8], tri, sm[:, 0, 0:8], bk.free, tld)
                P.mm(bk.t[:, 8:16], one, sm[:, 0, 0:8], start=False)
                t = P.mm(bk.t[:, 8:16], tri, sm[:, 1, 0:8], start=False, sig=True)
                yield
                f["gc"] = A.act(sm[:, :, 24:32], bk.t[:, 0:16].rearrange("p (a n) -> p a n", a=2), ACT.Copy, t)
                bk.done(f["gc"])
                f["be"] = t2
                f["ld"] = tld
            else:
                A.do(lambda e: e.preload_act_table_set(LNEXP), sig=False)
            tgc, tbe, tld = f["gc"], f["be"], f["ld"]
            for hh in range(0, 4, 2):
                bk = p.ps.get()
                P.wait(bk.free, tsl)
                for i in range(2):
                    for tt in range(2):
                        t = P.tr(bk.t[:, (i * 2 + tt) * 128:(i * 2 + tt + 1) * 128],
                                 vT[:, hh + i, tt * 128:(tt + 1) * 128], p.ident, sig=True)
                yield
                for i in range(2):
                    for tt in range(2):
                        tvb = V.ts(vb[:, tt, (hh + i) * 128:(hh + i + 1) * 128],
                                   bk.t[:, (i * 2 + tt) * 128:(i * 2 + tt + 1) * 128], beta(tt, hd + hh + i), None,
                                   MUL, None, t, tbe, prev)
                bk.done(tvb)
            fr = [None, None, None]
            nrm = {}

            def sq_(g):
                s = DT[:, (g % 3) * 512:(g % 3) * 512 + 512]
                x2 = qk[:, 2 * g:2 * g + 2, :].rearrange("p c n -> p (c n)")
                nrm[g] = s, x2, A.act(s, x2, ACT.Square, t1, fr[g % 3])

            def sum_(g):
                s, x2, t1_ = nrm[g]
                bk = p.ps.get()
                nrm[g] = s, x2, bk, P.mm(bk.t, one, s, t1_, bk.free, sig=True)

            def rs_(g):
                s, x2, bk, t = nrm[g]
                t3 = A.act(s, bk.t, ACT.Ln, t, bias=p.cst[:, C_EPS:C_EPS + 1])
                bk.done(t3)
                t4 = A.act(s, s, ACT.Exp, t3, scale=-0.5)
                fr[g % 3] = V.stt(x2, x2, SQ if g < 2 else 1.0, s, MUL, MUL, t4)

            yield from gskew(4, [sq_, sum_, rs_])
            tn = fr
            bb = {}

            def bcast(h):
                lb_ = Mx[:, (h % 2) * 512:(h % 2) * 512 + 256]
                bb_ = Mx[:, (h % 2) * 512 + 256:(h % 2) * 512 + 512]
                w = bb.get(h - 2, (None, None))[1]
                t0 = V.cp(lb_.rearrange("p (a n) -> p a n", a=2),
                          bc(sm[:, :, hd + h:hd + h + 1], [128, 2, 128]), tld, prev, w)
                t1_ = V.cp(bb_.rearrange("p (a n) -> p a n", a=2),
                           bc(sm[:, :, 8 + hd + h:9 + hd + h], [128, 2, 128]), prev, w, tbe)
                bb[h] = lb_, bb_, t0, t1_

            def spread(h):
                lb_, bb_, t0, t1_ = bb[h]
                bk = p.ps.get()
                P.mm(bk.t[:, 0:256], lb_[:, 0:128], p.cst[:, C_TRI:C_TRI + 256], bk.free, t0, t1_)
                P.mm(bk.t[:, 0:256], lb_[:, 128:256], p.cst[:, C_ZERO:C_ZERO + 256], start=False)
                for tt in range(2):
                    t = P.mm(bk.t[:, 256 + tt * 128:384 + tt * 128], bb_[:, tt * 128:(tt + 1) * 128], p.ident,
                             start=False, sig=True)
                bb[h] = bk, t

            def decays(h):
                bk, t = bb[h]
                d = h * 384
                V.ts(DT[:, d:d + 256], bk.t[:, 0:256], gcol(0, hd + h), 0.0, SUB, MIN, t, tgc, tn)
                V.ts(DT[:, d + 256:d + 384], bk.t[:, 128:256], gcol(1, hd + h), 0.0, SUB, MIN)
                f["kb"] = V.tt(kb[:, h * 256:(h + 1) * 256], qk[:, 4 + h, :], bk.t[:, 256:512], MUL, tn, prev)
                bk.done(f["kb"])

            yield from gskew(4, [bcast, spread, decays])
            te = A.act(DT, DT, ACT.Exp, V.now())
            yield
            d4 = DT.rearrange("p (h b t) -> p h b t", h=4, b=3)
            for bi in (0, 2):
                td = V.tt(d4[:, :, bi, :], d4[:, :, bi, :], bc(tri.unsqueeze(1), [128, 4, 128]), MUL, te)
            pr = {}

            def prods(i):
                h, w = i % 4, i // 4
                kT = qk[:, 4 + h, :]
                rhs = kb[:, h * 256:(h + 1) * 256] if w == 0 else qk[:, h, :]
                bk = p.ps.get()
                P.mm(bk.t[:, 0:256], kT[:, 0:128], rhs, bk.free, f["kb"], tn)
                t = P.mm(bk.t[:, 256:384], kT[:, 128:256], rhs[:, 128:256], start=False, sig=True)
                pr[i] = bk, t

            def decayed(i):
                h, w = i % 4, i // 4
                bk, t = pr[i]
                dst = LT if w == 0 else AT
                f["l", w] = V.tt(dst[:, h * 384:h * 384 + 384], bk.t[:, 0:384], DT[:, h * 384:h * 384 + 384], MUL,
                                 t, td, prev, tvb)
                bk.done(f["l", w])

            yield from gskew(8, [prods, decayed])
            tl = f["l", 0]
            L4 = LT.rearrange("p (h b t) -> p h b t", h=4, b=3)
            diag = lambda tt: L4[:, :, tt * 2, :]
            v4 = lambda ap, tt: ap.rearrange("p (h a t) -> p h a t", h=4, a=2)[:, :, tt, :]
            lev = lambda l: p.cst[:, C_LEV + l * 128:C_LEV + (l + 1) * 128]
            m4 = lambda l: bc(lev(l).unsqueeze(1), [128, 4, 128])
            for tt in range(2):
                t1 = V.tt(v4(Tt, tt), diag(tt), m4(0), MUL, tl, prev)
                t1 = V.tt(v4(Tt, tt), bc(p.ident.unsqueeze(1), [128, 4, 128]), v4(Tt, tt), SUB, t1)
            banks = []
            for g in range(2):
                bk = p.ps.get()
                P.wait(bk.free, t1)
                for i in range(4):
                    t = P.tr(bk.t[:, i * 128:(i + 1) * 128], inst_at(Tt, g * 4 + i), p.ident, sig=True)
                banks.append((bk, t))
            LM = DT[:, 0:1024]
            tm = [G.tt(v4(LM, tt), diag(tt), m4(1), MUL, tl, f["l", 1]) for tt in range(2)]
            yield
            tT = [None, None]
            for g, (bk, t) in enumerate(banks):
                tT[g] = A.act(Tm[:, g * 512:(g + 1) * 512], bk.t, ACT.Copy, t, prev)
                bk.done(tT[g])
            ttt = [t1, t1]
            for level in range(1, 7):
                bs_ = []
                for g in range(2):
                    bk = p.ps.get()
                    P.wait(bk.free, tm, tT[g])
                    for i in range(4):
                        t = P.mm(bk.t[:, i * 128:(i + 1) * 128], inst_at(LM, g * 4 + i), inst_at(Tm, g * 4 + i),
                                 start=(i == 0), sig=True)
                    bs_.append((bk, t))
                if level < 6:
                    tm = [G.tt(v4(LM, tt), diag(tt), m4(level + 1), MUL, tl, t) for tt in range(2)]
                yield
                tM = []
                for g, (bk, t) in enumerate(bs_):
                    tM.append(A.act(Mx[:, g * 512:(g + 1) * 512], bk.t, ACT.Copy, t))
                    bk.done(tM[g])
                for g in range(2):
                    b1 = p.ps.get()
                    b2 = p.ps.get() if level < 6 else None
                    P.wait(b1.free, b2.free if b2 else None, tM[g], ttt[g])
                    for i in range(4):
                        j = g * 4 + i
                        t = P.mm(b1.t[:, i * 128:(i + 1) * 128], inst_at(Mx, j), inst_at(Tt, j), start=(i == 0),
                                 sig=True)
                    if b2:
                        for i in range(4):
                            j = g * 4 + i
                            t = P.mm(b2.t[:, i * 128:(i + 1) * 128], inst_at(Tt, j), inst_at(Mx, j), start=(i == 0),
                                     sig=True)
                    yield
                    s = slice(g * 512, (g + 1) * 512)
                    ttt[g] = V.tt(Tt[:, s], Tt[:, s], b1.t, SUB, t)
                    b1.done(ttt[g])
                    if b2:
                        tT[g] = V.tt(Tm[:, s], Tm[:, s], b2.t, SUB, t)
                        b2.done(tT[g])
            U = Mx
            hsl = lambda h: slice(h * 128, (h + 1) * 128)
            bk = p.ps.get()
            P.wait(bk.free, ttt)
            for h in range(4):
                t = P.mm(bk.t[:, hsl(h)], inst_at(Tt, h * 2), vb[:, 0, hsl(h)], start=(h == 0), sig=True)
            yield
            t1 = A.act(U[:, 0:512], bk.t, ACT.Copy, t)
            bk.done(t1)
            bk = p.ps.get()
            P.wait(bk.free, t1)
            for h in range(4):
                t = P.mm(bk.t[:, hsl(h)], LT[:, h * 384 + 128:h * 384 + 256], U[:, hsl(h)], start=(h == 0), sig=True)
            yield
            t2_ = V.tt(vb[:, 1, :], vb[:, 1, :], bk.t, SUB, t)
            bk.done(t2_)
            bk = p.ps.get()
            P.wait(bk.free, t2_)
            for h in range(4):
                t = P.mm(bk.t[:, hsl(h)], inst_at(Tt, h * 2 + 1), vb[:, 1, hsl(h)], start=(h == 0), sig=True)
            yield
            t3 = A.act(U[:, 512:1024], bk.t, ACT.Copy, t)
            bk.done(t3)
            banks = []
            for tt in range(2):
                bk = p.ps.get()
                P.wait(bk.free, t1, t3, f["l", 1])
                for h in range(4):
                    d = h * 384
                    if tt == 0:
                        t = P.mm(bk.t[:, hsl(h)], AT[:, d:d + 128], U[:, hsl(h)], start=(h == 0), sig=True)
                    else:
                        P.mm(bk.t[:, hsl(h)], AT[:, d + 128:d + 256], U[:, hsl(h)], start=(h == 0), stop=False)
                        t = P.mm(bk.t[:, hsl(h)], AT[:, d + 256:d + 384], U[:, 512 + h * 128:640 + h * 128],
                                 start=False, sig=True)
                banks.append((bk, t))
            f["mid"] = t
            yield
            for tt, (bk, t) in enumerate(banks):
                to = A.act(vb[:, tt, :], bk.t, ACT.Copy, t)
                bk.done(to)
            yield from p.headnorm(vb, 4, 128, gn[:, 128:256], o, DT, to, tgs, tgn)
            for tt in range(2):
                t1 = V.cp(o[:, tt, :], vb[:, tt, :], p.hn)
            f["oa", 2 + H] = t1
            f["hg"] = [V.now(), A.now(), P.now()]

        tz0 = V.do(lambda e: e.memset(Z[:, :, 0:3], 0.0), bt)
        for H in range(2):
            for part in range(3):
                b, t = p.proj("ab_in", range((8 + part * 2 + H) * 4, (9 + part * 2 + H) * 4), "B", lt=lt)
                for h in range(2):
                    k = part * 4 + h * 2
                    tz = A.act(Z[:, k:k + 2, 3:259], view2(b[h]), ACT.Copy, t, f["z", part] if H else None)
                    b[h].done(tz)
                if H == 0:
                    p.bg(conv(0, [tz, tz0], (part,)), (1, 1))
            tg = blkA(14 + H, OA[2 + H])
            if H == 0:
                bs, t = p.proj_small("ab_small", 16, lt)
                tsm = A.act(p.sq[0:16, 0:256], bs.t[0:16, 0:256], ACT.Copy, t, p.dg_t)
                bs.done(tsm)
            p.finish()
            f.pop("mid", None)
            p.bg(gdn(H, [tz, tz0], tg, tsm), R3[0] if H == 0 else (1, 1))
            if H:
                for part in range(3):
                    f.pop(("z", part))
        for g in range(2):
            if g:
                while "mid" not in f:
                    p.step()
                A.wait(f["mid"])
            tq = blkB(g, Qs[g], 0 if g == 0 else None)
            tf = blkB(2 + g, Fs[g], 1 if g == 0 else None)
            p.rate = R3[1]
            tv = blkA(4 + g, Vs[g], 2 if g == 0 else None)
            tg = blkA(6 + g, OA[g])
            if g == 0:
                p.bg(hgrn(g, tq, tf, tv, tg), R3[1])
        p.finish()
        tproj = P.now()
        lts = {}
        for g in (2, 3, 0):
            p.run(p.turn(OA[g], 4 * g, 4, f["oa", g], tproj))
            for k in range(4 * g, 4 * g + 4):
                lts[k] = p.turned
            if g == 3:
                p.gpost = oall[:, 2048:4096]
                p.tpost = p.load("gbc", p.gpost, a["g_post01"], p.turned)
        p.bg(hgrn(1, tq, tf, tv, tg), R3[2])
        p.out_part("ab_out", [2, 3, 0], lts, dst=m)
        p.finish()
        p.run(p.turn(OA[1], 4, 4, f["oa", 1], tproj))
        for k in range(4, 8):
            lts[k] = p.turned
        p.out_part("ab_out", [1], lts, dst=m, last=True, first=False)
        p.post(m)


def layer4(p):
    V, A, P, G, a = p.V, p.A, p.P, p.G, p.a
    with ExitStack() as c:
        sb = lambda n, s: p.sb("l4" + n, s, F32, c)
        qT = sb("q", [128, 16, 256])
        ks = sb("ks", [128, 4, 256])
        kw = sb("kw", [128, 4, 256])
        vs = sb("vs", [128, 2, 512])
        vw = sb("vw", [128, 2, 512])
        gl = sb("gl", [128, 2, 48])
        dm = sb("dm", [128, 384 + 64])
        hT = sb("ht", [128, 128])
        kcm = sb("kcm", [128, 64])
        vcm = sb("vcm", [16, 512])
        SR = Ring([sb(f"s{i}", [128, 528])[:, :] for i in range(3)])
        PT = Ring([sb(f"pt{i}", [128, 640])[:, :] for i in range(2)])
        big = sb("big", [128, 8320])
        kc = big[:, 0:1024].rearrange("p (c n) -> p c n", c=4)
        vc = big[:, 1024:2048].rearrange("p (c n) -> p c n", c=4)
        rhs = big[:, 2048:3968]
        w1 = [big[:, 3968:6016], big[:, 6016:8064]]
        w2 = big[:, 8064:8320]
        m = big[:, 0:4096].rearrange("p (a n) -> p a n", a=2)
        p.gpost = big[:, 4096:6144]
        bt = p.barrier()
        tdm = p.load("dm4", dm[:, :], a["dist4"], bt)
        tw2 = p.load("w2", w2, a["cmp_w2"], bt)
        tw1 = [p.load(f"w1{i}", w1[i], a["cmp_w1"][i], bt) for i in range(2)]
        lt = p.norm_T("norm10")
        f = {}
        for i, dst in ((4, kc), (5, vc), (6, ks), (8, kw)):
            b, t = p.proj("nsa_in", range(i * 4, i * 4 + 4), "B", lt=lt)
            for h in range(2):
                f[i] = A.act(dst[:, 2 * h:2 * h + 2, :], view2(b[h]), ACT.Copy, t)
                b[h].done(f[i])
            if i == 5:
                p.bg(compress(p, f, kc, vc, rhs, w1, tw1, w2, tw2, hT, kcm, vcm), (1, 1))
        for i, dst in ((7, vs), (9, vw)):
            b, t = p.proj("nsa_in", range(i * 4, i * 4 + 4), "A", lt=lt)
            for tt in range(2):
                f[i] = A.act(dst[:, tt, :], b[tt].t, ACT.Copy, t)
                b[tt].done(f[i])
        bs, t = p.proj_small("nsa_small", 48, lt)
        tgl = A.act(p.sq[0:48, 0:256], bs.t[0:48, 0:256], ACT.Sigmoid, t, p.dg_t)
        bs.done(tgl)
        p.finish()
        tgl = p.tokens_first(48, gl[:, :, :], tgl)
        hold = {}

        def scores(it):
            h, qt = it // 2, it % 2
            g = h // 4
            nk = 128 * (qt + 1)
            q = qT[:, h, qt * 128:(qt + 1) * 128]
            b0, b1 = p.ps.get(), p.ps.get()
            P.wait(b0.free, b1.free, f["q", g], f[6], f[8], f["kc"])
            P.mm(b0.t[:, 0:nk], q, ks[:, g, 0:nk])
            P.mm(b0.t[:, 256:256 + nk], q, kw[:, g, 0:nk], start=False)
            t = P.mm(b1.t[:, 0:15], q, kcm[:, g * 15:(g + 1) * 15], sig=True)
            hold[it] = b0, b1, t

        def soft(it):
            h, qt = it // 2, it % 2
            nk = 128 * (qt + 1)
            b0, b1, t = hold[it]
            s = SR.get()
            mo = 128 if qt else 0
            d3 = bc(dm[:, mo:mo + nk].unsqueeze(1), [128, 2, nk])
            s3 = s.t[:, 0:2 * nk].rearrange("p (a n) -> p a n", a=2)
            p3 = b0.t.rearrange("p (a n) -> p a n", a=2)[:, :, 0:nk]
            t1 = V.stt(s3, d3, -SLOPE2[h], p3, MUL, ADD, t, tdm, s.free)
            b0.done(t1)
            sc = s.t[:, 512:527]
            t2 = V.stt(sc, dm[:, 384 + qt * 16:384 + qt * 16 + 15], -SLOPE2[h], b1.t[:, 0:15], MUL, ADD, t, s.free)
            b1.done(t2)
            mx, den = p.cell(3), p.cell(3)
            t3 = V.red(mx[:, 0:2], s3, MAX, t1)
            t4 = V.red(mx[:, 2:3], sc, MAX, t2)
            t5 = V.ts(mx, mx, -1.0, None, MUL, None, t3, t4)
            ap = [s.t[:, 0:nk], s.t[:, nk:2 * nk], sc]
            for i in range(3):
                t6 = A.act(ap[i], ap[i], ACT.Exp, t5, bias=mx[:, i:i + 1], acc=den[:, i:i + 1])
            hold[it] = s, den, t6, ap

        def gates(it):
            h, qt = it // 2, it % 2
            s, den, t6, ap = hold[it]
            nk = 128 * (qt + 1)
            rg = p.cell(3)
            t1 = V.rec(rg, den, t6)
            g3 = gl[:, qt, 3 * h:3 * h + 3]
            gw = [g3[:, 1:2], g3[:, 2:3], g3[:, 0:1]]
            for i in range(3):
                t2 = V.ts(ap[i], ap[i], rg[:, i:i + 1], gw[i], MUL, MUL, t1, tgl)
            v0 = 384 + 32 + qt * 16
            t3 = V.tt(ap[2], ap[2], dm[:, v0:v0 + 15], MUL, t2)
            hold[it] = s, t3, ap

        def turn_p(it):
            s, t3, ap = hold[it]
            n = 2 * (it % 2 + 1)
            b0, b1 = p.ps.get(), p.ps.get()
            P.wait(b0.free, b1.free, t3)
            for i in range(n):
                P.tr(b0.t[:, i * 128:(i + 1) * 128], s.t[:, i * 128:(i + 1) * 128], p.ident)
            t = P.tr(b1.t[0:15, 0:128], ap[2], p.ident, sig=True)
            s.done(t)
            hold[it] = b0, b1, t, n

        def moved(it):
            b0, b1, t, n = hold[it]
            pt = PT.get()
            t4 = A.act(pt.t[:, 0:n * 128], b0.t[:, 0:n * 128], ACT.Copy, t, pt.free)
            b0.done(t4)
            t5 = A.act(pt.t[0:15, 512:640], b1.t[0:15, 0:128], ACT.Copy, t)
            b1.done(t5)
            hold[it] = pt, t5, n

        def pv(it):
            h, qt = it // 2, it % 2
            g = h // 4
            pt, t5, n = hold[it]
            bk = p.ps.get()
            P.wait(bk.free, t5, f[7], f[9], f["vc"])
            gs = slice(g * 128, (g + 1) * 128)
            kt = qt + 1
            for i in range(n):
                src = vs if i < kt else vw
                P.mm(bk.t[:, 0:128], src[:, i % kt, gs], pt.t[:, i * 128:(i + 1) * 128], start=(i == 0), stop=False)
            t = P.mm(bk.t[:, 0:128], vcm[0:15, gs], pt.t[0:15, 512:640], start=False, sig=True)
            pt.done(t)
            hold[it] = bk, t

        def store(it):
            h, qt = it // 2, it % 2
            bk, t = hold[it]
            f["o", h] = A.act(qT[:, h, qt * 128:(qt + 1) * 128], bk.t[:, 0:128], ACT.Copy, t)
            bk.done(f["o", h])
            f["n"] = it

        def att():
            for t in range(32 * 2 + 5):
                for s_, fn in ((6, store), (5, moved), (5, pv), (1, soft), (4, turn_p), (0, scores), (3, gates)):
                    if t >= s_ and (t - s_) % 2 == 0 and (t - s_) // 2 < 32:
                        it = (t - s_) // 2
                        if s_ == 0:
                            while ("q", it // 8) not in f:
                                yield
                        fn(it)
                yield

        p.bg(att(), R4[0])
        for i in range(4):
            b, t = p.proj("nsa_in", range(i * 4, i * 4 + 4), "B", lt=lt)
            for h in range(2):
                k = i * 4 + 2 * h
                tq = A.act(qT[:, k:k + 2, :], view2(b[h]), ACT.Copy, t, scale=SQ)
                b[h].done(tq)
            f["q", i] = tq
        tproj = t
        lts = {}

        def heads(n):
            while f.get("n", 0) < 8 * n + 7:
                p.step()
            for k in range(4 * n, 4 * n + 4, 2):
                tk = p.to_lhs(qT[:, k:k + 2, :], k, 2, tproj, f["o", k + 1])
                lts[k] = lts[k + 1] = tk

        p.rate = R4[1]
        heads(0)
        A.wait(f["vc"])
        p.tpost = p.load("gbc", p.gpost, a["g_post11"], f["vc"])
        p.out_part("nsa_out", [0], lts, dst=m)
        heads(1)
        p.out_part("nsa_out", [1], lts, dst=m, first=False)
        heads(2)
        p.out_part("nsa_out", [2], lts, dst=m, first=False)
        heads(3)
        p.finish()
        p.out_part("nsa_out", [3], lts, dst=m, last=True, first=False)
        p.post(m)


def compress(p, f, kc, vc, rhs, w1, tw1, w2, tw2, hT, kcm, vcm):
    V, A, P, a = p.V, p.A, p.P, p.a
    r4 = rhs.rearrange("p (g j l) -> p g j l", g=4, j=15)
    rl = rhs.rearrange("p (n l) -> p l n", l=32)
    t = None
    for which, src in ((0, kc), (1, vc)):
        hv = hT[:, which * 64:which * 64 + 60]
        pos = p.c(f"pos{which}", 0, 32)
        for g in range(4):
            s3 = src[:, g, :].rearrange("p (j l) -> p j l", l=16)
            for half in range(2):
                tr = V.tt(r4[:, g, :, half * 16:half * 16 + 16], s3[:, half:half + 15, :],
                          bc(pos[:, half * 16:half * 16 + 16].unsqueeze(1), [128, 15, 16]), ADD, f[4 + which], t)
            yield
        bk = p.ps.get()
        P.wait(bk.free, tr)
        for half in range(2):
            P.wait(tw1[half])
            for l in range(16):
                ll = half * 16 + l
                t = P.mm(bk.t[:, 0:60], w1[half][:, l * 128:(l + 1) * 128], rl[:, ll, :], start=(ll == 0),
                         stop=(ll == 31), sig=(l % 4 == 3))
                if l % 4 == 3:
                    yield
            if which == 0:
                tw1[half] = p.load(f"w1{half}", w1[half], a["cmp_w1"][2 + half], t)
        th = A.act(hv, bk.t[:, 0:60], ACT.Silu, t)
        bk.done(th)
        bk = p.ps.get()
        P.wait(bk.free, th, tw2)
        if which == 0:
            t_ = P.mm(bk.t[:, 0:60], w2[:, 0:128], hv, sig=True)
            yield
            f["kc"] = A.act(kcm[:, 0:60], bk.t[:, 0:60], ACT.Copy, t_)
            bk.done(f["kc"])
        else:
            for g in range(4):
                t_ = P.mm(bk.t[0:15, g * 128:(g + 1) * 128], hv[:, g * 15:(g + 1) * 15], w2[:, 128:256],
                          start=(g == 0), sig=True)
            yield
            f["vc"] = A.act(vcm[0:15, :], bk.t[0:15, :], ACT.Copy, t_)
            bk.done(f["vc"])


def schedule(parts):
    out = []

    def tiles(name, r):
        for t in r:
            out.extend([(name, t, 0, HALF, TILE), (name, t, HALF, HALF, TILE)])

    def blocks(name, bs):
        for b in bs:
            tiles(name, range(4 * b, 4 * b + 4))

    def small(name, n):
        out.append((name, None, 0, 16 * n, 16 * n))

    def outs(name, ks):
        for part in ks:
            for nb in range(4):
                tiles(name, [nb * 4 + k for k in part])

    for part in parts:
        if part == "1":
            blocks("ev_in", [0, 1, 2, 3, 4, 5, 15, 12, 13, 14, 6, 7, 8, 9, 10, 11])
            outs("ev_out", [[0, 1, 2], [3]])
        if part == "2":
            blocks("od_in", [0, 1])
            small("od_alr", 16)
            blocks("od_in", [2, 3, 8, 9, 4, 5, 6, 7, 10, 11])
            outs("od_out", [[0, 1], [2, 3]])
        if part == "3":
            blocks("ab_in", [8, 10, 12, 14])
            small("ab_small", 16)
            blocks("ab_in", [9, 11, 13, 15, 0, 2, 4, 6, 1, 3, 5, 7])
            outs("ab_out", [[2, 3, 0], [1]])
        if part == "4":
            blocks("nsa_in", [4, 5, 6, 8, 7, 9])
            small("nsa_small", 48)
            blocks("nsa_in", [0, 1, 2, 3])
            outs("nsa_out", [[0], [1], [2], [3]])
        if part in ("f0", "f1"):
            for half, bs in enumerate((range(0, 6), range(6, 11))):
                for nb in bs:
                    blocks("ffn_gu" + part[1], [nb, 11 + nb])
                for nb in range(4):
                    tiles("ffn_down" + part[1], range(nb * 11 + half * 6, nb * 11 + half * 6 + len(bs)))
    return out


def build(nc, a, out, parts=("1", "2", "n", "3", "f0", "4", "f1")):
    with ExitStack() as ctx:
        p = Program(nc, ctx, a, schedule(parts))
        xv = a["x"][0].rearrange("(t p) d -> p t d", p=128)
        for h in range(2):
            hs = slice(h * 1024, (h + 1) * 1024)
            t = p.load(f"x{h}", p.x[:, :, hs], xv[:, :, hs], eng=p.S)
            for tt in range(2):
                p.xt[tt] += [t, t]
        p.cst_t = [p.load("cst", p.cst[:, :], a["cst"], eng=p.S), p.load("cst", p.col[:, :], a["col"], eng=p.S)]
        p.square_all()
        for e in (p.V, p.A, p.P):
            e.wait(p.cst_t)
        for part in parts:
            if part == "n":
                continue
            if part == "2":
                layer2(p, "n" in parts)
            elif part in ("f0", "f1"):
                p.ffn(int(part[1]), part, last=(part == "f1"))
            else:
                {"1": layer1, "3": layer3, "4": layer4}[part](p)
        ov = out[0].rearrange("(t p) d -> p t d", p=128)
        for nb in range(4):
            ns = slice(nb * 512, (nb + 1) * 512)
            t = p.load("out", ov[:, :, ns], p.x[:, :, ns], p.xt[0][nb], p.xt[1][nb], eng=p.S)
        p.S.wait(t)
        block = ctx.enter_context(nc.Block())

        def play(engine):
            def run(e):
                for f in engine.list:
                    f(e)
            return run

        block.sync(play(p.S))
        block.scalar(play(p.A))
        block.vector(play(p.V))
        block.gpsimd(play(p.G))
        block.tensor(play(p.P))


def arrange(i):
    def tiles(w, cols=None):
        k, n = w.shape
        return np.ascontiguousarray(w.reshape(k // 512, 4, 128, n // 512, 512).transpose(3, 0, 2, 1, 4)
                                    .reshape(-1, 128, TILE))

    def small(w):
        return np.ascontiguousarray(w.reshape(16, 128, -1).transpose(1, 0, 2).reshape(128, -1))

    def cols(v):
        return v.reshape(-1, 128).T

    def rows(v):
        return np.ascontiguousarray(np.broadcast_to(v.reshape(1, -1), (128, v.size)))

    f = {k: np.asarray(v) for k, v in i.items()}
    d = {"x": f["x"], "cst": constants(), "dist": distances()}
    dist = d["dist"]
    d["dist4"] = np.ascontiguousarray(dist[:, M_C:M_N])
    ev = f["ev_w_in"][0]
    d["ev_in"] = tiles(ev)
    d["ev_out"] = tiles(f["ev_w_out"][0])
    d["ev_wa"] = np.ascontiguousarray(f["ev_w_a"][0].transpose(1, 0, 2).reshape(128, -1))
    d["ev_wi"] = np.ascontiguousarray(f["ev_w_i"][0].transpose(1, 0, 2).reshape(128, -1))
    od = f["od_w_in"][0]
    d["od_in"] = tiles(np.concatenate([od[:, 0:2048], od[:, 2064:6160]], axis=1))
    d["od_alr"] = small(od[:, 2048:2064])
    d["od_out"] = tiles(f["od_w_out"][0])
    d["w_alpha"] = f["od_w_alpha"][0]
    d["head_norm"] = rows(f["od_head_norm"][0])
    d["v_norm"] = rows(f["od_v_norm"][0])
    d["w_s"] = np.ascontiguousarray(f["od_w_s"][0].transpose(2, 0, 1).reshape(128, -1))
    d["final_norm"] = rows(f["final_norm"])
    ab = f["ab_w_in_2"][0]
    d["ab_in"] = tiles(ab[:, 0:8192])
    d["ab_small"] = small(ab[:, 8192:8208])
    d["ab_out"] = tiles(f["ab_w_out_2"][0])
    d["gn3"] = rows(np.concatenate([f["hgrn_norm_g_2"][0], f["gdn_norm_g_2"][0]]))
    ns = f["nsa_w_in_2"][0]
    d["nsa_in"] = tiles(ns[:, 0:5120])
    d["nsa_small"] = small(ns[:, 5120:5168])
    d["nsa_out"] = tiles(f["nsa_w_out_2"][0])
    d["cmp_w1"] = np.ascontiguousarray(f["nsa_cmp_w1_2"][0].reshape(2, 2, 16, 128, 128).transpose(0, 1, 3, 2, 4)
                                       .reshape(4, 128, TILE))
    d["cmp_w2"] = np.ascontiguousarray(f["nsa_cmp_w2_2"][0].transpose(1, 0, 2).reshape(128, -1))
    for l in range(2):
        d[f"ffn_gu{l}"] = tiles(f["ffn_w_gu_2"][l])
        d[f"ffn_down{l}"] = tiles(f["ffn_w_down_2"][l])
    for l in range(2):
        for n in (1, 3):
            d[f"g_post{l}{n}"] = rows(f["norm_g_2"][l, n])
    c = {"ev_norm": cols(f["ev_norm"][0]), "ev_conv_w": cols(f["ev_conv_w"][0]), "ev_conv_b": cols(f["ev_conv_b"][0]),
         "ev_b_a": cols(f["ev_b_a"][0]), "ev_b_i": cols(f["ev_b_i"][0]), "ev_lam": cols(f["ev_lam"][0]),
         "od_norm": cols(f["od_norm"][0]), "od_b_alpha": cols(f["od_b_alpha"][0]), "od_b_s": cols(f["od_b_s"][0]),
         "norm00": cols(f["norm_g_2"][0, 0]), "norm02": cols(f["norm_g_2"][0, 2]),
         "norm10": cols(f["norm_g_2"][1, 0]), "norm12": cols(f["norm_g_2"][1, 2]),
         "gdn_conv": cols(f["gdn_conv_w_2"][0]), "lb": cols(f["hgrn_lb_logits_2"][0]),
         "a_log": rows(f["gdn_a_log_2"][0]), "dt_bias": rows(f["gdn_dt_bias_2"][0]),
         "pos0": f["nsa_cmp_pos_2"][0, 0].T, "pos1": f["nsa_cmp_pos_2"][0, 1].T}
    d["col"] = np.ascontiguousarray(np.concatenate([c[k] for k, _ in COLS], axis=1))
    return d


def kernel(**inputs):
    import concourse.bacc as _bacc
    from concourse.bass_utils import run_bass_kernel_spmd as _run

    nc = _bacc.Bacc("TRN2", target_bir_lowering=False, num_devices=1)
    arrays, a = {}, {}
    for name, v in arrange(inputs).items():
        arrays["in_" + name] = v
        a[name] = nc.dram_tensor("in_" + name, v.shape, mybir.dt.from_np(v.dtype), kind="ExternalInput").ap()
    out = nc.dram_tensor("out_y", (1, 256, D), F32, kind="ExternalOutput").ap()
    build(nc, a, out)
    r = _run(nc, [arrays], core_ids=[0])
    return r.results[0]["out_y"]
```
